# Optimizing a Trainium2 kernel written in Bass

```python
import math
import jax
import jax.numpy as jnp
from jax import lax
import numpy as np

D_MODEL = 1024
BATCH = 1
SEQ = 1024
DEPTH = 1
DEC_BATCH = 8
DEC_SEQ = 4
PAST_LEN = 1024
PAGE_SIZE = 128

HEAD_DIM = 128
HEADS_PER_GROUP = 4
GROUP_WINDOWS = (128, 512, 2048)
GROUP_DILATIONS = (1, 4, 16)
N_GROUPS = 3
N_HEADS_A = N_GROUPS * HEADS_PER_GROUP
ATT_WIDTH = N_HEADS_A * HEAD_DIM
MERGE_WIDTH = HEADS_PER_GROUP * HEAD_DIM
ATT_SCALE = HEAD_DIM ** -0.5
LRU_WIDTH = D_MODEL
LRU_BLOCKS = 16
LRU_BLOCK = LRU_WIDTH // LRU_BLOCKS
CONV_WIDTH = 4
RG_C = 8.0
D_FF = 4 * D_MODEL
PLE_DIM = 256
REL_BUCKETS = 32
REL_MAX_DIST = 2048
NORM_EPS = 1e-6
NEG_INF = -1e30
SPLITS = (ATT_WIDTH, 2 * ATT_WIDTH, 3 * ATT_WIDTH, 3 * ATT_WIDTH + LRU_WIDTH,
          3 * ATT_WIDTH + 2 * LRU_WIDTH, 3 * ATT_WIDTH + 2 * LRU_WIDTH + D_MODEL)
IN_WIDTH = 3 * ATT_WIDTH + 2 * LRU_WIDTH + 2 * D_MODEL

kernel_name = 'dilated_swa_rglru_hybrid_step'

def _rms_norm(x, gain):
    x32 = x.astype(jnp.float32)
    y = x32 * lax.rsqrt(jnp.mean(x32 * x32, axis=-1, keepdims=True) + NORM_EPS)
    return (y * gain.astype(jnp.float32)).astype(x.dtype)

def _softmax_lse(logits):
    m = jnp.max(logits, axis=-1, keepdims=True)
    p = jnp.exp(logits - m)
    s = jnp.sum(p, axis=-1, keepdims=True)
    return p / s, (m + jnp.log(s))[..., 0]

def _t5_bucket(dist):
    max_exact = REL_BUCKETS // 2
    d = jnp.maximum(dist, 1).astype(jnp.float32)
    large = max_exact + (jnp.log(d / max_exact) / math.log(REL_MAX_DIST / max_exact)
                         * (REL_BUCKETS - max_exact)).astype(jnp.int32)
    large = jnp.minimum(large, REL_BUCKETS - 1)
    return jnp.where(dist < max_exact, dist, large)

def _slot_bias(rel_bias, g):
    dil, win = GROUP_DILATIONS[g], GROUP_WINDOWS[g]
    dist = dil * jnp.arange(win // dil + 1, dtype=jnp.int32)
    hs = slice(g * HEADS_PER_GROUP, (g + 1) * HEADS_PER_GROUP)
    return rel_bias[_t5_bucket(dist)][:, hs].astype(jnp.float32)

def _band_dilated_attention(q, k, v, bias, dil, win):
    bsz, seq, nh, hd = q.shape
    qb = win // dil
    span = dil * qb
    s_pad = -(-seq // span) * span
    n_blk = s_pad // span
    m_len = s_pad // dil

    def to_blocks(t):
        t = jnp.pad(t, ((0, 0), (0, s_pad - seq), (0, 0), (0, 0)))
        t = t.reshape(bsz, m_len, dil, nh, hd).transpose(0, 2, 1, 3, 4)
        return t.reshape(bsz, dil, n_blk, qb, nh, hd)

    def with_prev(t):
        prev = jnp.pad(t, ((0, 0), (0, 0), (1, 0), (0, 0), (0, 0), (0, 0)))[:, :, :-1]
        return jnp.concatenate([prev, t], axis=3)

    qs = to_blocks(q)
    ks = with_prev(to_blocks(k))
    vs = with_prev(to_blocks(v))
    iq = jnp.arange(qb)[:, None]
    ik = jnp.arange(2 * qb)[None, :]
    slot = qb + iq - ik
    in_band = (slot >= 0) & (slot <= qb)
    has_key = (jnp.arange(n_blk)[:, None, None] > 0) | (ik >= qb)[None]
    mask = in_band[None, None] & has_key[:, None]
    band_bias = jnp.transpose(bias[jnp.clip(slot, 0, qb)], (2, 0, 1))
    logits = jnp.einsum('brnqhd,brnkhd->brnhqk', qs, ks) * ATT_SCALE + band_bias
    probs, lse = _softmax_lse(jnp.where(mask, logits, NEG_INF))
    o = jnp.einsum('brnhqk,brnkhd->brnqhd', probs, vs)
    o = o.reshape(bsz, dil, m_len, nh, hd).transpose(0, 2, 1, 3, 4).reshape(bsz, s_pad, nh, hd)[:, :seq]
    lse = jnp.swapaxes(lse, 3, 4).reshape(bsz, dil, m_len, nh).transpose(0, 2, 1, 3)
    lse = lse.reshape(bsz, s_pad, nh)[:, :seq]
    return o, lse

def _gather_dilated_attention(q, k_all, v_all, bias, dil, win, n_buf):
    t = q.shape[1]
    nk = win // dil + 1
    idx = n_buf + jnp.arange(t)[:, None] - dil * jnp.arange(nk)[None, :]
    valid = idx >= 0
    idx_c = jnp.maximum(idx, 0)
    kg = k_all[:, idx_c]
    vg = v_all[:, idx_c]
    logits = jnp.einsum('bthd,btkhd->bthk', q, kg) * ATT_SCALE + bias.T
    probs, lse = _softmax_lse(jnp.where(valid[None, :, None, :], logits, NEG_INF))
    o = jnp.einsum('bthk,btkhd->bthd', probs, vg)
    return o, lse

def _combine_groups(outs, lses):
    w = jax.nn.softmax(jnp.stack(lses, 0), axis=0)
    return jnp.sum(w[..., None] * jnp.stack(outs, 0), axis=0)

def _prompt_attend(q, k, v, biases):
    outs, lses, rows = [], [], []
    f32 = jnp.float32
    for g in range(N_GROUPS):
        hs = slice(g * HEADS_PER_GROUP, (g + 1) * HEADS_PER_GROUP)
        qg, kg, vg = q[:, :, hs], k[:, :, hs], v[:, :, hs]
        o, lse = _band_dilated_attention(qg.astype(f32), kg.astype(f32), vg.astype(f32), biases[g],
                                         GROUP_DILATIONS[g], GROUP_WINDOWS[g])
        outs.append(o)
        lses.append(lse)
        keep = min(GROUP_WINDOWS[g], q.shape[1])
        rows.append(jnp.stack([kg, vg], axis=2)[:, -keep:])
    return _combine_groups(outs, lses), rows

def _sample_attend(q, k, v, biases, bufs):
    outs, lses, rows = [], [], []
    f32 = jnp.float32
    for g in range(N_GROUPS):
        hs = slice(g * HEADS_PER_GROUP, (g + 1) * HEADS_PER_GROUP)
        qg, kg, vg = q[:, :, hs], k[:, :, hs], v[:, :, hs]
        buf = bufs[g]
        k_all = jnp.concatenate([buf[:, :, 0].astype(kg.dtype), kg], axis=1)
        v_all = jnp.concatenate([buf[:, :, 1].astype(vg.dtype), vg], axis=1)
        o, lse = _gather_dilated_attention(qg.astype(f32), k_all.astype(f32), v_all.astype(f32), biases[g],
                                           GROUP_DILATIONS[g], GROUP_WINDOWS[g], buf.shape[1])
        outs.append(o)
        lses.append(lse)
        rows.append(jnp.stack([kg, vg], axis=2))
    return _combine_groups(outs, lses), rows

def _lin_combine(left, right):
    a1, b1 = left
    a2, b2 = right
    return a1 * a2, a2 * b1 + b2

def _conv_rglru(xb, conv_prev, h0, w_conv, b_conv, w_rg_a, b_rg_a, w_rg_i, b_rg_i, lam):
    t = xb.shape[1]
    xcat = jnp.concatenate([conv_prev.astype(xb.dtype), xb], axis=1)
    xc = b_conv
    for j in range(CONV_WIDTH):
        xc = xc + w_conv[j] * xcat[:, j:j + t]
    new_conv = xcat[:, t:]
    x32 = xc.astype(jnp.float32)
    xblk = x32.reshape(x32.shape[0], t, LRU_BLOCKS, LRU_BLOCK)
    r = jax.nn.sigmoid(jnp.einsum('btni,nij->btnj', xblk, w_rg_a.astype(jnp.float32)).reshape(x32.shape) + b_rg_a)
    i = jax.nn.sigmoid(jnp.einsum('btni,nij->btnj', xblk, w_rg_i.astype(jnp.float32)).reshape(x32.shape) + b_rg_i)
    log_a = RG_C * r * jax.nn.log_sigmoid(lam.astype(jnp.float32))
    a = jnp.exp(log_a)
    b = jnp.sqrt(-jnp.expm1(2.0 * log_a)) * (i * x32)
    b = b.at[:, 0].add(a[:, 0] * h0)
    _, h = lax.associative_scan(_lin_combine, (a, b), axis=1)
    return h, new_conv, h[:, -1]

def _layer(x, pe, attend, conv_prev, h0, g_mix, w_in, g_q, g_k, w_oa, w_conv, b_conv, w_rg_a, b_rg_a,
           w_rg_i, b_rg_i, lam, w_ob, w_o, g_mlp, w_up, w_down, g_ple, w_ple_gate, w_ple_in):
    bsz, t = x.shape[0], x.shape[1]
    h = _rms_norm(x, g_mix)
    q, k, v, xb, yb, ga, gb = jnp.split(h @ w_in, SPLITS, axis=-1)
    q = _rms_norm(q.reshape(bsz, t, N_HEADS_A, HEAD_DIM), g_q)
    k = _rms_norm(k.reshape(bsz, t, N_HEADS_A, HEAD_DIM), g_k)
    v = v.reshape(bsz, t, N_HEADS_A, HEAD_DIM)
    att, kv_rows = attend(q, k, v)
    a_out = att.reshape(bsz, t, MERGE_WIDTH).astype(x.dtype) @ w_oa
    hr, conv_new, h_last = _conv_rglru(xb, conv_prev, h0, w_conv, b_conv, w_rg_a, b_rg_a, w_rg_i, b_rg_i, lam)
    b_out = (hr.astype(x.dtype) * jax.nn.gelu(yb)) @ w_ob
    x = x + (jax.nn.sigmoid(ga) * a_out + jax.nn.sigmoid(gb) * b_out) @ w_o
    x = x + jnp.square(jax.nn.relu(_rms_norm(x, g_mlp) @ w_up)) @ w_down
    x = x + jax.nn.sigmoid(_rms_norm(x, g_ple) @ w_ple_gate) * (pe @ w_ple_in)
    return x, kv_rows, conv_new, h_last

def setup_inputs(seed: int = 0) -> dict:
    key = jax.random.key(seed)
    k = jax.random.split(key, 32)
    f32 = jnp.float32

    def nrm(i, shape, scale):
        return scale * jax.random.normal(k[i], shape, f32)

    wb = [min(w, PAST_LEN) for w in GROUP_WINDOWS]
    u = jax.random.uniform(k[31], (DEPTH, LRU_WIDTH), f32, 0.9, 0.999)
    return {
        'x_prompt': nrm(0, (BATCH, SEQ, D_MODEL), 1.0),
        'x_sample': nrm(1, (DEC_BATCH, DEC_SEQ, D_MODEL), 1.0),
        'p_prompt': nrm(2, (DEPTH, BATCH, SEQ, PLE_DIM), 1.0),
        'p_sample': nrm(3, (DEPTH, DEC_BATCH, DEC_SEQ, PLE_DIM), 1.0),
        'cache_kv1': nrm(4, (DEPTH, DEC_BATCH, wb[0], 2, HEADS_PER_GROUP, HEAD_DIM), 1.0),
        'cache_kv2': nrm(5, (DEPTH, DEC_BATCH, wb[1], 2, HEADS_PER_GROUP, HEAD_DIM), 1.0),
        'cache_kv3': nrm(6, (DEPTH, DEC_BATCH, wb[2], 2, HEADS_PER_GROUP, HEAD_DIM), 1.0),
        'state_conv': nrm(7, (DEPTH, DEC_BATCH, CONV_WIDTH - 1, LRU_WIDTH), 1.0),
        'state_lru': nrm(8, (DEPTH, DEC_BATCH, LRU_WIDTH), 0.5),
        'rel_bias': nrm(9, (REL_BUCKETS, N_HEADS_A), 0.5),
        'g_mix': 1.0 + nrm(10, (DEPTH, D_MODEL), 0.05),
        'w_in': nrm(11, (DEPTH, D_MODEL, IN_WIDTH), D_MODEL ** -0.5),
        'g_q': 1.0 + nrm(12, (DEPTH, HEAD_DIM), 0.05),
        'g_k': 1.0 + nrm(13, (DEPTH, HEAD_DIM), 0.05),
        'w_oa': nrm(14, (DEPTH, MERGE_WIDTH, D_MODEL), MERGE_WIDTH ** -0.5),
        'w_conv': nrm(15, (DEPTH, CONV_WIDTH, LRU_WIDTH), CONV_WIDTH ** -0.5),
        'b_conv': nrm(16, (DEPTH, LRU_WIDTH), 0.05),
        'w_rg_a': nrm(17, (DEPTH, LRU_BLOCKS, LRU_BLOCK, LRU_BLOCK), LRU_BLOCK ** -0.5),
        'b_rg_a': nrm(18, (DEPTH, LRU_WIDTH), 0.1),
        'w_rg_i': nrm(19, (DEPTH, LRU_BLOCKS, LRU_BLOCK, LRU_BLOCK), LRU_BLOCK ** -0.5),
        'b_rg_i': nrm(20, (DEPTH, LRU_WIDTH), 0.1),
        'lam': jnp.log(u) - jnp.log1p(-u),
        'w_ob': nrm(21, (DEPTH, LRU_WIDTH, D_MODEL), LRU_WIDTH ** -0.5),
        'w_o': nrm(22, (DEPTH, D_MODEL, D_MODEL), D_MODEL ** -0.5),
        'g_mlp': 1.0 + nrm(23, (DEPTH, D_MODEL), 0.05),
        'w_up': nrm(24, (DEPTH, D_MODEL, D_FF), D_MODEL ** -0.5),
        'w_down': nrm(25, (DEPTH, D_FF, D_MODEL), D_FF ** -0.5),
        'g_ple': 1.0 + nrm(26, (DEPTH, D_MODEL), 0.05),
        'w_ple_gate': nrm(27, (DEPTH, D_MODEL, D_MODEL), D_MODEL ** -0.5),
        'w_ple_in': nrm(28, (DEPTH, PLE_DIM, D_MODEL), PLE_DIM ** -0.5),
    }

def reference(x_prompt, x_sample, p_prompt, p_sample, cache_kv1, cache_kv2, cache_kv3, state_conv, state_lru,
              rel_bias, g_mix, w_in, g_q, g_k, w_oa, w_conv, b_conv, w_rg_a, b_rg_a, w_rg_i, b_rg_i, lam,
              w_ob, w_o, g_mlp, w_up, w_down, g_ple, w_ple_gate, w_ple_in):
    biases = [_slot_bias(rel_bias, g) for g in range(N_GROUPS)]
    yp, ys = x_prompt, x_sample
    kvp = [[], [], []]
    kvs = [[], [], []]
    convp, lrup, convs, lrus = [], [], [], []
    for i in range(DEPTH):
        lp = (g_mix[i], w_in[i], g_q[i], g_k[i], w_oa[i], w_conv[i], b_conv[i], w_rg_a[i], b_rg_a[i],
              w_rg_i[i], b_rg_i[i], lam[i], w_ob[i], w_o[i], g_mlp[i], w_up[i], w_down[i], g_ple[i],
              w_ple_gate[i], w_ple_in[i])
        conv0 = jnp.zeros((yp.shape[0], CONV_WIDTH - 1, LRU_WIDTH), yp.dtype)
        h00 = jnp.zeros((yp.shape[0], LRU_WIDTH), jnp.float32)
        yp, rows_p, c_p, h_p = _layer(yp, p_prompt[i], lambda q, k, v: _prompt_attend(q, k, v, biases),
                                      conv0, h00, *lp)
        bufs = (cache_kv1[i], cache_kv2[i], cache_kv3[i])
        ys, rows_s, c_s, h_s = _layer(ys, p_sample[i], lambda q, k, v: _sample_attend(q, k, v, biases, bufs),
                                      state_conv[i], state_lru[i].astype(jnp.float32), *lp)
        for g in range(N_GROUPS):
            kvp[g].append(rows_p[g])
            kvs[g].append(rows_s[g])
        convp.append(c_p)
        lrup.append(h_p)
        convs.append(c_s)
        lrus.append(h_s)
    kv1_p, kv2_p, kv3_p = jnp.stack(kvp[0]), jnp.stack(kvp[1]), jnp.stack(kvp[2])
    kv1_s, kv2_s, kv3_s = jnp.stack(kvs[0]), jnp.stack(kvs[1]), jnp.stack(kvs[2])
    conv_p, lru_p = jnp.stack(convp), jnp.stack(lrup)
    conv_s, lru_s = jnp.stack(convs), jnp.stack(lrus)
    return (yp, ys, kv1_p, kv2_p, kv3_p, conv_p, lru_p, kv1_s, kv2_s, kv3_s, conv_s, lru_s)


_drawn_inputs = setup_inputs


def setup_inputs(seed=0):
    import zlib

    import numpy as np

    out = dict(_drawn_inputs(seed))
    spreads = {}
    factors = {'g_q': 8.0, 'g_ple': 22.247}
    for name, (base, spread) in spreads.items():
        noise = np.random.default_rng([zlib.crc32(name.encode()), seed]).standard_normal(out[name].shape)
        drawn = base * np.exp(spread * noise) if base else spread * noise
        out[name] = jnp.asarray(drawn.astype(out[name].dtype))
    for name, factor in factors.items():
        out[name] = (out[name] * factor).astype(out[name].dtype)
    return out
```

```python
import math
from contextlib import ExitStack

import numpy as np

import concourse.bass as bass
from concourse import mybir

ALU = mybir.AluOpType
ACT = mybir.ActivationFunctionType
F32 = mybir.dt.float32
F32R = mybir.dt.float32r
AX_X = mybir.AxisListType.X

P = 128
D = 1024
KD = D // P
NP_ = 1024
DB, DS = 8, 4
NS = DB * DS
T = NP_ + NS
NCH = 3
CH = T // NCH
HD = 128
HG = 4
NG = 3
DIL = (1, 4, 16)
STRIDE = (1, 4, 8)
CK = (128, 128, 128)
CSLOT = (DB, NS, NS // 2)
NT = NP_ // P
TL = NT
EPS = 1e-6
SCALE = HD ** -0.5
NEG = -1e30
BUCKETS = 32
MAXD = 2048
TOEP = 384
SB = DS + P
TB = TOEP + DS * SB
VEC = {"g_mix": 0, "g_mlp": 8, "g_ple": 16, "b_conv": 24, "b_a": 32, "b_i": 40, "lam": 48, "w_conv": 56}
NVEC = 88
BUMP = 16
PAIRS = 5
SLOTS = 9


def t5_bucket(dist):
    exact = BUCKETS // 2
    if dist < exact:
        return dist
    big = exact + int(np.float32(math.log(dist / exact) / math.log(MAXD / exact) * (BUCKETS - exact)))
    return min(big, BUCKETS - 1)


def bias_selection():
    sel = np.zeros((BUCKETS + 1, NG, TB), np.float32)
    for g, dil in enumerate(DIL):
        def fill(at, slot):
            if slot is None:
                sel[BUCKETS, g, at] = NEG
            else:
                sel[t5_bucket(dil * slot), g, at] = 1.0
        for j in range(TOEP):
            slot = 2 * P - 1 - j
            if g == 2:
                fill(j, slot // 2 if slot >= 0 and slot % 2 == 0 else None)
            else:
                fill(j, slot if 0 <= slot <= P else None)
        for t in range(DS):
            base = TOEP + t * SB
            for u in range(DS):
                seen = u <= t if g == 0 else u == t
                fill(base + u, t - u if seen else None)
            for c in range(P):
                if g == 2:
                    slot = CK[g] // 2 - c % (CK[g] // 2) if c // (CK[g] // 2) == t % 2 else 0
                else:
                    slot = P + t - c if g == 0 else CK[g] - c
                fill(base + DS + c, slot if 0 < slot <= P else None)
    return sel


def build(nc, a):
    with ExitStack() as ctx:
        cursor = [16512]

        def alloc(name, shape, dt=F32):
            size = 4 * int(np.prod(shape[1:]))
            t = nc.alloc_sbuf_tensor_at(name, list(shape), dt, offset=cursor[0])
            cursor[0] += (size + 31) // 32 * 32
            return t

        ident_at = cursor[0]
        ident = alloc("ident", [P, P])
        ones = alloc("ones", [P, P])
        vec = alloc("vec", [P, NVEC])
        clam = alloc("clam", [P, KD])
        c_eps = alloc("c_eps", [P, 1])
        act_at = cursor[0]
        act_hi_flat = alloc("act_hi", [P, KD * T + P - NS], F32R)
        act_lo_flat = alloc("act_lo", [P, KD * T + P - NS], F32R)
        act_hi = act_hi_flat[:, 0:KD * T].rearrange("p (k t) -> p k t", t=T)
        act_lo = act_lo_flat[:, 0:KD * T].rearrange("p (k t) -> p k t", t=T)
        phase_base = cursor[0]

        def sem(name):
            return ctx.enter_context(nc.semaphore(name))

        def vcol(name, k):
            return vec[:, VEC[name] + k:VEC[name] + k + 1]

        bias_dram = nc.dram_tensor("bias_dram", (NG, HG, TB), F32, kind="Internal").ap()
        table_dram = nc.dram_tensor("table_dram", (NG, HG, P, TOEP), F32, kind="Internal").ap()
        lse_dram = nc.dram_tensor("lse_dram", (NG * SLOTS, P), F32, kind="Internal").ap()
        att_dram = nc.dram_tensor("att_dram", (HG + 1, P, T), F32, kind="Internal").ap()

        shared = dict(
            cursor=cursor, alloc=alloc, sem=sem, vcol=vcol, ident=ident, ident_at=ident_at, ones=ones, vec=vec, clam=clam,
            c_eps=c_eps, act_at=act_at, act_hi=act_hi, act_lo=act_lo, act_hi_flat=act_hi_flat, act_lo_flat=act_lo_flat,
            bias_dram=bias_dram, table_dram=table_dram, lse_dram=lse_dram, att_dram=att_dram)
        prepare(nc, ctx, a, shared)
        cursor[0] = phase_base
        attention(nc, ctx, a, shared)
        cursor[0] = phase_base
        dense(nc, ctx, a, shared)


def prepare(nc, ctx, a, shared):
    alloc, sem, ident, ones, vec, clam, c_eps = \
        shared["alloc"], shared["sem"], shared["ident"], shared["ones"], shared["vec"], shared["clam"], shared["c_eps"]
    act_hi, act_lo, vcol, bias_dram, table_dram = shared["act_hi"], shared["act_lo"], shared["vcol"], shared["bias_dram"], shared["table_dram"]
    table_stored = sem("table_stored")
    x = alloc("x_in", [P, KD, T])
    sq = alloc("x_sq", [P, 2, T])
    ssum = alloc("x_ssum", [P, T])
    rstd = alloc("x_rstd", [P, T])
    hbuf = alloc("x_h", [P, 2, T])
    sel = alloc("bias_sel", [BUCKETS + 1, NG, TB])
    relb = alloc("relb", [BUCKETS + 1, NG * HG])
    brow = alloc("bias_rows", [HG, NG, TB])
    lt = alloc("lam_tmp", [P, 6, KD])
    HTB = TB // 2

    x_loaded, sel_loaded = [sem(f"x_loaded{k}") for k in range(KD)], sem("sel_loaded")
    const_done, relb_done = sem("const_done"), sem("relb_done")
    sq_done, sum_done, tot_psum, root_done, rstd_done = (sem(n) for n in ("sq_done", "sum_done", "tot_psum", "root_done", "rstd_done"))
    h_done, hi_done, lo_done, lo_odd_done = sem("h_done"), sem("hi_done"), sem("lo_done"), sem("lo_odd_done")
    bias_psum, bias_copied, bias_stored = sem("bias_psum"), sem("bias_copied"), sem("bias_stored")
    lam_a, lam_v, pad_done = sem("lam_a"), sem("lam_v"), sem("pad_done")

    with nc.psum_tensor("prep_tot", [P, NCH, 512], F32) as tot, nc.psum_tensor("prep_bias", [P, 2, 512], F32) as pb, \
            nc.Block() as block:

        @block.sync
        def _(sp):
            for k in range(KD):
                sp.dma_start(x[:, k], a["x_t"][:, k]).then_inc(x_loaded[k], 16)
                if k == 0:
                    sp.dma_start(vec[:], a["vecs"]).then_inc(sel_loaded, 16)
                    sp.dma_start(sel[:], a["bias_sel"]).then_inc(sel_loaded, 16)
                    sp.dma_start(relb[0:BUCKETS, :], a["rel_bias"]).then_inc(sel_loaded, 16)
            for g in range(NG):
                sp.wait_ge(bias_copied, 2 * (g + 1))
                sp.dma_start(bias_dram[g], brow[:, g, :]).then_inc(bias_stored, 16)
            sp.wait_ge(bias_stored, 16 * NG)
            for g in range(NG):
                for h in range(HG):
                    row = bias_dram[g, h]
                    src = bass.AP(row.tensor, row.offset, [[0, P], [1, TOEP]])
                    sp.dma_start(table_dram[g, h], src).then_inc(table_stored, 16)
            sp.wait_ge(table_stored, 16 * NG * HG)

        @block.gpsimd
        def _(pool):
            for padded in (shared["act_hi_flat"], shared["act_lo_flat"]):
                pool.memset(padded[:, KD * T:].bitcast(F32), 0.0).then_inc(pad_done, 1)
            pool.memset(ident[:], 0.0).then_inc(const_done, 1)
            pool.memset(ones[:], 1.0).then_inc(const_done, 1)
            pool.memset(c_eps[:], EPS).then_inc(const_done, 1)
            pool.wait_ge(const_done, 3)
            pool.memset(relb[BUCKETS:BUCKETS + 1, :], 1.0).then_inc(relb_done, 1)
            pool.wait_ge(relb_done, 1)
            pool.affine_select(out=ident[:], in_=ident[:], compare_op=ALU.not_equal, fill=1.0, base=0,
                               pattern=[[-1, P]], channel_multiplier=1).then_inc(const_done, 1)
            for k in range(0, KD, 2):
                pool.wait_ge(hi_done, k + 1)
                pool.tensor_tensor(act_lo[:, k], hbuf[:, k % 2], act_hi[:, k].bitcast(F32), ALU.subtract).then_inc(lo_done, 1)

        @block.scalar
        def _(act):
            act.wait_ge(sel_loaded, 16 * 3)
            act.activation(lt[:, 0], vec[:, VEC["lam"]:VEC["lam"] + KD], ACT.Abs).then_inc(lam_a, 1)
            act.wait_ge(lam_a, 1)
            act.activation(lt[:, 1], lt[:, 0], ACT.Exp, scale=-1.0).then_inc(lam_a, 1)
            for k in range(KD):
                act.wait_ge(x_loaded[k], 16)
                if k >= 2:
                    act.wait_ge(sum_done, k - 1)
                act.activation(sq[:, k % 2], x[:, k], ACT.Square).then_inc(sq_done, 1)
            act.wait_ge(const_done, 4)
            for c in range(NCH):
                act.wait_ge(tot_psum, c + 1)
                act.activation(rstd[:, c * CH:(c + 1) * CH], tot[:, c, 0:CH], ACT.Sqrt, bias=c_eps[:], scale=1.0 / D).then_inc(root_done, 1)
            for k in range(KD):
                act.wait_ge(h_done, k + 1)
                act.activation(act_hi[:, k], hbuf[:, k % 2], ACT.Copy).then_inc(hi_done, 1)

        @block.vector
        def _(dve):
            dve.wait_ge(lam_a, 2)
            n = [0]

            def chain(ins):
                n[0] += 1
                ins.then_inc(lam_v, 1)
                dve.wait_ge(lam_v, n[0])

            y, z, z2, acc = lt[:, 1], lt[:, 2], lt[:, 3], lt[:, 4]
            chain(dve.tensor_scalar(z2, y, 2.0, None, ALU.add))
            chain(dve.reciprocal(acc, z2))
            chain(dve.tensor_tensor(z, y, acc, ALU.mult))
            chain(dve.tensor_tensor(z2, z, z, ALU.mult))
            chain(dve.tensor_scalar(acc, z2, 1.0 / 17, 1.0 / 15, ALU.mult, ALU.add))
            for odd in (13, 11, 9, 7, 5, 3, 1):
                chain(dve.tensor_tensor(acc, acc, z2, ALU.mult))
                chain(dve.tensor_scalar(acc, acc, 1.0 / odd, None, ALU.add))
            chain(dve.tensor_tensor(acc, acc, z, ALU.mult))
            chain(dve.tensor_scalar(lt[:, 5], vec[:, VEC["lam"]:VEC["lam"] + KD], 0.0, 8.0, ALU.min, ALU.mult))
            chain(dve.tensor_scalar(acc, acc, -16.0, None, ALU.mult))
            chain(dve.tensor_tensor(clam[:], lt[:, 5], acc, ALU.add))
            for k in range(KD):
                dve.wait_ge(sq_done, k + 1)
                if k == 0:
                    dve.tensor_copy(ssum[:], sq[:, 0]).then_inc(sum_done, 1)
                else:
                    dve.wait_ge(sum_done, k)
                    dve.tensor_tensor(ssum[:], ssum[:], sq[:, k % 2], ALU.add).then_inc(sum_done, 1)
            for g in range(NG):
                for c in range(2):
                    dve.wait_ge(bias_psum, 2 * g + c + 1)
                    dve.tensor_copy(brow[:, g, c * HTB:(c + 1) * HTB], pb[0:HG, c, 0:HTB]).then_inc(bias_copied, 1)
            for c in range(NCH):
                dve.wait_ge(root_done, c + 1)
                dve.reciprocal(rstd[:, c * CH:(c + 1) * CH], rstd[:, c * CH:(c + 1) * CH]).then_inc(rstd_done, 1)
            dve.wait_ge(rstd_done, NCH)
            for k in range(KD + 1):
                if k < KD:
                    if k >= 2 and k % 2 == 0:
                        dve.wait_ge(lo_done, k // 2)
                    if k >= 2 and k % 2 == 1:
                        dve.wait_ge(lo_odd_done, k // 2)
                    dve.scalar_tensor_tensor(out=hbuf[:, k % 2], in0=x[:, k], scalar=vcol("g_mix", k), in1=rstd[:],
                                             op0=ALU.mult, op1=ALU.mult).then_inc(h_done, 1)
                if k and k % 2 == 0:
                    dve.wait_ge(hi_done, k)
                    dve.tensor_tensor(act_lo[:, k - 1], hbuf[:, 1], act_hi[:, k - 1].bitcast(F32), ALU.subtract).then_inc(lo_odd_done, 1)
            dve.wait_ge(lo_done, KD // 2)
            dve.wait_ge(lo_odd_done, KD // 2)

        @block.tensor
        def _(pe):
            pe.wait_ge(const_done, 4)
            pe.wait_ge(relb_done, 1)
            pe.wait_ge(sel_loaded, 16 * 3)
            for g in range(NG):
                for c in range(2):
                    if g:
                        pe.wait_ge(bias_copied, 2 * g - 1 + c)
                    pe.matmul(pb[0:HG, c, 0:HTB], relb[:, HG * g:HG * (g + 1)], sel[:, g, c * HTB:(c + 1) * HTB],
                              start=True, stop=True).then_inc(bias_psum, 1)
            pe.wait_ge(sum_done, KD)
            for c in range(NCH):
                pe.matmul(tot[:, c, 0:CH], ones[:], ssum[:, c * CH:(c + 1) * CH], start=True, stop=True).then_inc(tot_psum, 1)


def attention(nc, ctx, a, shared):
    alloc, sem, ident = shared["alloc"], shared["sem"], shared["ident"]
    act_hi, act_lo, c_eps = shared["act_hi_flat"], shared["act_lo_flat"], shared["c_eps"]
    bias_dram, lse_dram, att_dram = shared["bias_dram"], shared["lse_dram"], shared["att_dram"]

    w_raw = alloc("qkv_raw", [P, KD, 3 * HD])
    w_hi = alloc("qkv_hi", [P, KD, 3 * HD], F32R)
    w_lo = alloc("qkv_lo", [P, KD, 3 * HD], F32R)
    gq = alloc("gq", [P, HD])
    gk = alloc("gk", [P, HD])
    qk = alloc("qk_ring", [P, 3, 2, HD])
    ktok = alloc("ktok", [P, SLOTS, HD])
    qk_sq = alloc("qk_sq", [P, 2, HD])
    ss = alloc("qk_ss", [P, 3, 2])
    power = alloc("power", [P, 2])
    eps_sum = alloc("eps_sum", [P, 2])
    v = [alloc(f"v{g}", [P, SLOTS, HD]) for g in range(NG)]
    qkt = [alloc(f"qkt{g}", [P, 2, T]) for g in range(NG)]
    kc_at = shared["cursor"][0]
    kc = alloc("kcache", [P, 2, 8, P])
    vc = nc.alloc_sbuf_tensor_at("vcache", [P, 16, HD], F32, offset=kc_at)
    bias = alloc("bias", [P, 2 * P])
    bias_s = alloc("bias_s", [NS, NS + P])
    bias_n = alloc("bias_n", [NS, DS])
    same_seq = alloc("same_seq", [NS, NS])
    lt_s = alloc("lt_s", [P, NS])
    L = alloc("L", [P, 2, 2, 2 * P])
    pt = alloc("pt", [P, 4, P])
    nmax = alloc("nmax", [P, 2])
    rsum = alloc("rsum", [P, 2])
    m_all = alloc("m_all", [P, NG * SLOTS])
    s_all = alloc("s_all", [P, NG * SLOTS])
    lse = alloc("lse", [P, NG * SLOTS])
    lse_row = alloc("lse_row", [NG * SLOTS, P])
    o = [alloc(f"o{g}", [P, T]) for g in range(NG)]
    o0 = alloc("o0_kept", [P, T])
    e_at = shared["cursor"][0]
    e = alloc("e_bc", [P, NG, T])
    vc2 = nc.alloc_sbuf_tensor_at("vcache2", [P, 16, HD], F32, offset=e_at)
    mx = alloc("mx", [P, T])
    assert shared["cursor"][0] <= 229344, shared["cursor"][0]

    S = {}
    for n in ("w_loaded bias_loaded kc0_loaded kc1_loaded vc_loaded a_stored b_stored lse_stored e_loaded "
              "att_stored once init init2 whi wlo proj tok_copied sq_done eps_added stats normed qkt_psum qkt_ready "
              "s_psum newb max_done nmax_done exp_done rcp_done p_norm pt_psum pt_ready o_psum o_ready lt_ready "
              "kc_used lns lse_done lse_psum lse_copied o0_saved mx_a mxd sub ex prod den_a den rec comb_a comb_b "
              "comb").split():
        S[n] = sem("at_" + n)

    with nc.Block() as bump:
        @bump.sync
        def _(sp):
            for x in S.values():
                sp.sem_inc(x, BUMP)

    def tile_cols(src, k, g, i):
        if i == TL:
            return src[:, k * T + NP_:k * T + NP_ + P]
        pr = src[:, k * T:k * T + NP_]
        if g == 0:
            return pr[:, i * P:(i + 1) * P]
        if g == 1:
            return pr.rearrange("p (n m r) -> p r n m", n=2, r=4)[:, i // 2, i % 2]
        return pr.rearrange("p (m r) -> p r m", r=8)[:, i]

    def rows(i):
        return P if i < TL else NS

    def token_order(t, g):
        pr = t[:, 0:NP_]
        return pr if g == 0 else pr.rearrange("p (r m) -> p m r", r=STRIDE[g])

    def group_order(t, g):
        pr = t[:, 0:NP_]
        return pr if g == 0 else pr.rearrange("p (m r) -> p r m", r=STRIDE[g])

    def shaped(t, g, order):
        pr = t[:, 0:NP_]
        if g == 0:
            return pr
        return pr.rearrange("p (m r) -> p m r", r=STRIDE[g]) if order == "token" else pr.rearrange("p (r m) -> p r m", r=STRIDE[g])

    A_DMAS = (2, 2, 2)
    BIAS_DMAS = (3, 3, 3)
    V_DMAS = (1, 2, 1)

    def total(per_group, j, g):
        return sum(per_group) * j + sum(per_group[:g + 1])

    def keys(g, u):
        prev = (g == 0 and u > 0) or (g == 1 and u % 2 == 1)
        return (u - 1, 2) if prev else (u, 1)

    def pair_units(p):
        return (2 * p, 2 * p + 1) if p < PAIRS - 1 else (TL,)

    def blocks(g, p):
        out = []
        for x, u in enumerate(pair_units(p)):
            first, n = keys(g, u)
            out += [(x, u, b, first + b, n) for b in range(n)]
        return out

    def following(j, g):
        return (j, g + 1) if g < 2 else (j + 1, 0)

    def lagging(cur, nxt, i, lag):
        if nxt is None:
            if i - lag >= 0:
                return None
            q = (HG - 1) * 3 + 3
            return 9 * q + i - lag, cur, i - lag + SLOTS
        q = 3 * nxt[0] + nxt[1]
        if i - lag >= 0:
            return 9 * q + i - lag, nxt, i - lag
        if cur is None:
            return None
        return 9 * q + i - lag, cur, i - lag + SLOTS

    def walk(eng, body):
        for i in range(SLOTS):
            body(None, (0, 0), i)
        with eng.Fori(0, HG - 1, 1) as j:
            for g in range(NG):
                for i in range(SLOTS):
                    body((j, g), following(j, g), i)
        for g in range(NG):
            for i in range(SLOTS):
                body((HG - 1, g), following(HG - 1, g) if g < 2 else None, i)

    with ExitStack() as pctx:
        def bank(n):
            return pctx.enter_context(nc.psum_tensor("at_" + n, [P, 512], F32))

        pj = [bank("proj0"), bank("proj1"), bank("proj2")]
        ptq, pS, pPT, pO, pX = bank("qkt"), bank("s"), bank("pt"), bank("o"), bank("x")
        pLT, pSS, pLSE = pX[:, 0:NS], pX[0:NS, P:2 * P + NS], pX[0:NG * SLOTS, 384:512]
        block = pctx.enter_context(nc.Block())

        @block.sync
        def _(sp):
            sp.dma_start(w_raw[:], a["w_qkv"][0]).then_inc(S["w_loaded"], 16)
            sp.dma_start(gq[:], a["g_q"].partition_broadcast(P)).then_inc(S["once"], 16)
            sp.dma_start(gk[:], a["g_k"].partition_broadcast(P)).then_inc(S["once"], 16)
            sp.dma_start(same_seq[:], a["same_seq"]).then_inc(S["once"], 16)

            def load_bias(j, g):
                sp.wait_ge(S["max_done"], BUMP + PAIRS * (3 * j + g))
                hd = bias_dram[g, j]
                table = shared["table_dram"][g, j]
                table = bass.AP(table.tensor, table.offset + P - 1, [[TOEP - 1, P], [1, 2 * P]])
                sp.dma_start(bias[:], table).then_inc(S["bias_loaded"], 16)
                row = bass.AP(hd.tensor, hd.offset + TOEP, [[0, DB], [SB, DS], [1, DS]])
                sp.dma_start(bias_n[:], row).then_inc(S["bias_loaded"], 16)
                row = bass.AP(hd.tensor, hd.offset + TOEP + DS, [[0, DB], [SB, DS], [1, P]])
                sp.dma_start(bias_s[:, NS:NS + P], row).then_inc(S["bias_loaded"], 16)

            def load_cache(j, g, i):
                s = 3 * j + g
                if i < 4:
                    n = CSLOT[g] // 4
                    sp.wait_ge(S["kc_used"], BUMP + 4 * s + i - 1)
                    sp.wait_ge(S["o_psum"], BUMP + PAIRS * s)
                    sp.dma_start(kc[:, i % 2, 0:n, 0:CK[g]], a[f"kc{g}"][j, :, n * i:n * (i + 1)]).then_inc(S[f"kc{i % 2}_loaded"], 16)
                if i == 3 and CSLOT[g] > 16:
                    sp.wait_ge(S["prod"], BUMP + 3 * (j + 1))
                    sp.wait_ge(S["den"], BUMP + j + 1)
                    sp.dma_start(vc2[0:CK[g]], a[f"vc{g}"][j, :, 16:32]).then_inc(S["vc_loaded"], 16)
                if i == 6:
                    sp.wait_ge(S["kc_used"], BUMP + 4 * (s + 1))
                    n = min(16, CSLOT[g])
                    sp.dma_start(vc[0:CK[g], 0:n], a[f"vc{g}"][j, :, 0:n]).then_inc(S["vc_loaded"], 16)

            def store_prompt_kv(j, g):
                q = 3 * j + g
                sp.wait_ge(S["normed"], BUMP + 9 * q + NT)
                kv = a[f"kv{g}_p"][:, :, j, :]
                for c, t in ((0, ktok), (1, v[g])):
                    if g == 0:
                        sp.dma_start(kv[:, c], t[:, NT - 1]).then_inc(S["a_stored"], 16)
                    elif g == 1:
                        sp.dma_start(kv[:, c].rearrange("(m r) d -> m r d", r=4),
                                     t[:, 0:NT].rearrange("p (r n) d -> p r n d", n=2)[:, :, 1]).then_inc(S["a_stored"], 16)
                    else:
                        sp.dma_start(kv[:, c].rearrange("(m r) d -> m r d", r=8), t[:, 0:NT]).then_inc(S["a_stored"], 16)

            def store_sample_kv(j, g):
                q = 3 * j + g
                sp.wait_ge(S["normed"], BUMP + 9 * q + SLOTS)
                for c, t in ((0, ktok), (1, v[g])):
                    sp.dma_start(a[f"kv{g}_s"][:, c, j, :], t[0:NS, TL]).then_inc(S["b_stored"], 16)

            def load_weights(ij):
                sp.wait_ge(S["lse_copied"], BUMP + ij + 1)
                sp.dma_start(lse_dram, lse_row[:]).then_inc(S["lse_stored"], 16)
                sp.wait_ge(S["lse_stored"], BUMP + 16 * (ij + 1))
                sp.wait_ge(S["o_psum"], BUMP + PAIRS * 3 * ij)
                for g in range(NG):
                    sp.dma_start(e[:, g], bass.AP(lse_dram.tensor, lse_dram.offset + g * SLOTS * P, [[0, P], [1, T]])).then_inc(S["e_loaded"], 16)

            def body(cur, nxt, i):
                if nxt is not None and i == 0:
                    q = 3 * nxt[0] + nxt[1]
                    if not (type(nxt[0]) is int and nxt == (HG - 1, 2)):
                        sp.wait_ge(S["wlo"], BUMP + 8 * (q + 1))
                        nj, ng = following(*nxt)
                        sp.dma_start(w_raw[:], a["w_qkv"][3 * nj + ng]).then_inc(S["w_loaded"], 16)
                if cur is not None:
                    j, g = cur
                    if i == 0:
                        store_sample_kv(j, g)
                        load_bias(j, g)
                    if i == 1 and g == 0:
                        load_weights(j)
                    if i == 4 and g == 1:
                        sp.wait_ge(S["comb"], BUMP + j + 1)
                        sp.dma_start(att_dram[j], o0[:]).then_inc(S["att_stored"], 16)
                    if i < 4 or i == 6:
                        load_cache(j, g, i)
                if nxt is not None and i == SLOTS - 1:
                    store_prompt_kv(*nxt)

            walk(sp, body)
            load_weights(HG)
            sp.wait_ge(S["comb"], BUMP + HG + 1)
            sp.dma_start(att_dram[HG], o0[:]).then_inc(S["att_stored"], 16)
            sp.wait_ge(S["att_stored"], BUMP + 16 * (HG + 1))
            sp.wait_ge(S["a_stored"], BUMP + 16 * total(A_DMAS, HG - 1, 2))
            sp.wait_ge(S["b_stored"], BUMP + 16 * (2 * 3 * HG))

        @block.gpsimd
        def _(pool):
            pool.memset(m_all[:], 0.0).then_inc(S["init"], 1)
            pool.memset(power[:], -0.5).then_inc(S["init"], 1)
            pool.memset(eps_sum[:], HD * EPS).then_inc(S["init"], 1)
            pool.memset(s_all[:], 1.0).then_inc(S["init"], 1)
            for g in range(NG):
                pool.memset(o[g][:], 0.0).then_inc(S["init"], 1)
            pool.memset(L[:], 0.0).then_inc(S["init"], 1)
            pool.memset(ktok[:], 0.0).then_inc(S["init"], 1)

            def inverse_rms(n, i):
                r, sl = rows(i), i % 3
                pool.wait_ge(S["sq_done"], BUMP + n + 1)
                pool.tensor_tensor(ss[0:r, sl], ss[0:r, sl], eps_sum[0:r], ALU.add).then_inc(S["eps_added"], 1)
                pool.wait_ge(S["eps_added"], BUMP + n + 1)
                pool.tensor_tensor(ss[0:r, sl], ss[0:r, sl], power[0:r], ALU.pow).then_inc(S["stats"], 1)

            def less_max(ij, g):
                if g == 0:
                    pool.wait_ge(S["mxd"], BUMP + ij + 1)
                    pool.wait_ge(S["e_loaded"], BUMP + 16 * (3 * (ij + 1)))
                    pool.tensor_tensor(e[:, 0], e[:, 0], mx[:], ALU.subtract).then_inc(S["sub"], 1)
                else:
                    eg = shaped(e[:, g], g, "group")
                    pool.tensor_tensor(eg, eg, group_order(mx, g), ALU.subtract).then_inc(S["sub"], 1)
                    pool.tensor_tensor(e[:, g, NP_:T], e[:, g, NP_:T], mx[:, NP_:T], ALU.subtract).then_inc(S["sub"], 1)

            def weigh(ij, g):
                if g == 0:
                    pool.wait_ge(S["ex"], BUMP + ij + 1)
                    pool.wait_ge(S["o0_saved"], BUMP + ij + 1)
                dst = o0 if g == 0 else o[g]
                pool.tensor_tensor(dst[:], dst[:], e[:, g], ALU.mult).then_inc(S["prod"], 1)

            def body(cur, nxt, i):
                if nxt is not None:
                    inverse_rms(9 * (3 * nxt[0] + nxt[1]) + i, i)
                if cur is not None:
                    j, g = cur
                    if g == 0 and 4 <= i <= 6:
                        less_max(j, i - 4)
                    if g == 0 and 7 <= i:
                        weigh(j, i - 7)
                    if g == 1 and i == 0:
                        weigh(j, 2)

            pool.wait_ge(S["init"], BUMP + 9)
            walk(pool, body)
            for g in range(NG):
                weigh(HG, g)

        @block.scalar
        def _(act):
            def split_hi(q):
                act.wait_ge(S["w_loaded"], BUMP + 16 * (q + 1))
                act.wait_ge(S["proj"], BUMP + 9 * q)
                for k in range(KD):
                    act.activation(w_hi[:, k], w_raw[:, k], ACT.Copy).then_inc(S["whi"], 1)

            def copy_qkt(tau, step, i):
                g, r = step[1], rows(i)
                q = 3 * step[0] + g
                act.wait_ge(S["qkt_psum"], BUMP + tau + 1)
                act.wait_ge(S["s_psum"], BUMP + PAIRS * (q - 2))
                act.wait_ge(S["kc_used"], BUMP + 4 * (q - 2))
                src = ptq[:, 0:2 * P].rearrange("p (c t) -> p c t", c=2)[:, :, 0:r]
                act.activation(qkt[g][:, :, i * P:i * P + r], src, ACT.Copy).then_inc(S["qkt_ready"], 1)

            def row_stats(n, i):
                r, sl = rows(i), i % 3
                act.wait_ge(S["tok_copied"], BUMP + n + 1)
                act.wait_ge(S["normed"], BUMP + n - 2)
                act.activation(qk_sq[0:r, 0], qk[0:r, sl, 0], ACT.Square, accum_out=ss[0:r, sl, 0:1])
                act.activation(qk_sq[0:r, 1], qk[0:r, sl, 1], ACT.Square, accum_out=ss[0:r, sl, 1:2]).then_inc(S["sq_done"], 1)

            def exps(j, g, p):
                s = 3 * j + g
                act.wait_ge(S["nmax_done"], BUMP + PAIRS * s + p + 1)
                for x, u in enumerate(pair_units(p)):
                    r = rows(u)
                    n = keys(g, u)[1] * P if u < TL else NS + CK[g]
                    l = L[0:r, p % 2, x, 0:n]
                    col = g * SLOTS + u
                    ins = act.activation(l, l, ACT.Exp, bias=nmax[0:r, x:x + 1], accum_out=s_all[0:r, col:col + 1])
                ins.then_inc(S["exp_done"], 1)

            def copy_pt(j, g, p):
                n = PAIRS * (3 * j + g) + p
                act.wait_ge(S["pt_psum"], BUMP + n + 1)
                act.wait_ge(S["o_psum"], BUMP + n)
                if p < PAIRS - 1:
                    nb = len(blocks(g, p))
                    ins = act.activation(pt[:, 0:nb], pPT[:, 0:nb * P].rearrange("p (b q) -> p b q", q=P), ACT.Copy)
                else:
                    act.activation(pt[0:CK[g], 0, 0:NS], pPT[0:CK[g], 0:NS], ACT.Copy)
                    ins = act.activation(pt[0:NS, 1, 0:NS], pPT[0:NS, P:P + NS], ACT.Copy)
                ins.then_inc(S["pt_ready"], 1)

            def log_sums(ij):
                act.wait_ge(S["exp_done"], BUMP + 15 * ij)
                act.wait_ge(S["lse_psum"], BUMP + ij)
                act.activation(lse[:], s_all[:], ACT.Ln).then_inc(S["lns"], 1)
                act.wait_ge(S["comb"], BUMP + ij)
                act.wait_ge(S["att_stored"], BUMP + 16 * ij)
                act.wait_ge(S["o_ready"], BUMP + 15 * ij)
                act.activation(o0[:], o[0][:], ACT.Copy).then_inc(S["o0_saved"], 1)

            def weights(ij):
                act.wait_ge(S["sub"], BUMP + 5 * (ij + 1))
                act.activation(e[:], e[:], ACT.Exp).then_inc(S["ex"], 1)

            def body(cur, nxt, i):
                if nxt is not None and i == 0:
                    split_hi(3 * nxt[0] + nxt[1])
                if cur is not None and 0 <= i - 4:
                    copy_pt(*cur, i - 4)
                lag = lagging(cur, nxt, i, 3)
                if lag is not None:
                    copy_qkt(*lag)
                if nxt is not None:
                    row_stats(9 * (3 * nxt[0] + nxt[1]) + i, i)
                if cur is not None:
                    if 0 <= i - 2 < PAIRS:
                        exps(*cur, i - 2)
                    if i == 5:
                        s = 3 * cur[0] + cur[1]
                        ck = CK[cur[1]]
                        act.wait_ge(S["kc_used"], BUMP + 4 * (s + 1))
                        act.wait_ge(S["s_psum"], BUMP + PAIRS * s)
                        act.activation(lt_s[0:ck], pLT[0:ck], ACT.Copy).then_inc(S["lt_ready"], 1)
                    if cur[1] == 0 and i == 0:
                        log_sums(cur[0])
                    if cur[1] == 0 and i == 7:
                        weights(cur[0])

            act.wait_ge(S["init"], BUMP + 9)
            walk(act, body)
            log_sums(HG)
            weights(HG)

        @block.vector
        def _(dve):
            def split_lo(q):
                dve.wait_ge(S["proj"], BUMP + 9 * q)
                for k in range(KD):
                    dve.wait_ge(S["whi"], BUMP + 8 * q + k + 1)
                    dve.tensor_tensor(w_lo[:, k], w_raw[:, k], w_hi[:, k].bitcast(F32), ALU.subtract).then_inc(S["wlo"], 1)

            def scale_probs(j, g, p):
                n = PAIRS * (3 * j + g) + p
                us = pair_units(p)
                r, col = rows(us[0]), g * SLOTS + us[0]
                dve.wait_ge(S["exp_done"], BUMP + n + 1)
                dve.reciprocal(rsum[0:r, 0:len(us)], s_all[0:r, col:col + len(us)]).then_inc(S["rcp_done"], 1)
                dve.wait_ge(S["rcp_done"], BUMP + n + 1)
                for x, u in enumerate(us):
                    nk = keys(g, u)[1] * P if u < TL else NS + CK[g]
                    l = L[0:r, p % 2, x, 0:nk]
                    ins = dve.tensor_scalar(l, l, rsum[0:r, x:x + 1], None, ALU.mult)
                ins.then_inc(S["p_norm"], 1)

            def normalise(tau, step, i):
                j, g = step
                q = 3 * j + g
                r, sl = rows(i), i % 3
                dve.wait_ge(S["stats"], BUMP + tau + 1)
                if i == 0:
                    dve.wait_ge(S["a_stored"], BUMP + 16 * (total(A_DMAS, j, g) - A_DMAS[g]))
                if i == TL:
                    dve.wait_ge(S["b_stored"], BUMP + 16 * (2 * q))
                dve.scalar_tensor_tensor(out=qk[0:r, sl, 0], in0=qk[0:r, sl, 0], scalar=ss[0:r, sl, 0:1],
                                         in1=gq[0:r], op0=ALU.mult, op1=ALU.mult)
                dve.scalar_tensor_tensor(out=ktok[0:r, i], in0=qk[0:r, sl, 1], scalar=ss[0:r, sl, 1:2],
                                         in1=gk[0:r], op0=ALU.mult, op1=ALU.mult).then_inc(S["normed"], 1)

            def copy_tile(n, g, i):
                r, sl = rows(i), i % 3
                dve.wait_ge(S["proj"], BUMP + n + 1)
                dve.wait_ge(S["qkt_psum"], BUMP + n - 2)
                dve.tensor_copy(qk[0:r, sl], pj[sl][0:r, 0:2 * P].rearrange("p (c d) -> p c d", c=2))
                dve.tensor_copy(v[g][0:r, i], pj[sl][0:r, 2 * P:3 * P]).then_inc(S["tok_copied"], 1)

            def maxima(j, g, p):
                s = 3 * j + g
                n = PAIRS * s + p
                us = pair_units(p)
                if p == 0:
                    dve.wait_ge(S["bias_loaded"], BUMP + 16 * total(BIAS_DMAS, j, g))
                    new = bias_s[:, 0:NS].rearrange("p (b t) -> p b t", t=DS)
                    dve.tensor_tensor(new, bias_n[:].unsqueeze(1).to_broadcast([NS, DB, DS]),
                                      same_seq[:].rearrange("p (b t) -> p b t", t=DS), ALU.add).then_inc(S["newb"], 1)
                    dve.wait_ge(S["newb"], BUMP + s + 1)
                dve.wait_ge(S["s_psum"], BUMP + n + 1)
                dve.wait_ge(S["pt_psum"], BUMP + (PAIRS * s if p == 0 else n - 1))
                dve.wait_ge(S["exp_done"], BUMP + n)
                dve.memset(nmax[:], 0.0)
                for x, u in enumerate(us):
                    r, nb = rows(u), keys(g, u)[1]
                    if u == TL:
                        nk, src, b = NS + CK[g], pSS, bias_s
                        src, b = pSS[:, 0:nk], bias_s[:, 0:nk]
                    else:
                        nk = nb * P
                        src = pS[:, x * 256:x * 256 + nk]
                        b = bias[:, 2 * P - nk:2 * P]
                    col = g * SLOTS + u
                    ins = dve.tensor_tensor_reduce(L[0:r, p % 2, x, 0:nk], src, b, 1.0, -3.0e38, ALU.add, ALU.max,
                                                   m_all[0:r, col:col + 1])
                ins.then_inc(S["max_done"], 1)
                dve.wait_ge(S["max_done"], BUMP + n + 1)
                r, col = rows(us[0]), g * SLOTS + us[0]
                dve.tensor_scalar(nmax[0:r, 0:len(us)], m_all[0:r, col:col + len(us)], -1.0, None, ALU.mult).then_inc(S["nmax_done"], 1)

            def copy_out(j, g, p):
                n = PAIRS * (3 * j + g) + p
                dve.wait_ge(S["o_psum"], BUMP + n + 1)
                if p == 0:
                    if g == 0:
                        dve.wait_ge(S["o0_saved"], BUMP + j + 1)
                w = 2 * P if p < PAIRS - 1 else NS
                dve.tensor_copy(o[g][:, p * 2 * P:p * 2 * P + w], pO[:, 0:w]).then_inc(S["o_ready"], 1)

            def lse_rows(ij):
                dve.wait_ge(S["lns"], BUMP + ij + 1)
                dve.tensor_tensor(lse[:], lse[:], m_all[:], ALU.add).then_inc(S["lse_done"], 1)
                dve.wait_ge(S["lse_psum"], BUMP + ij + 1)
                dve.wait_ge(S["lse_stored"], BUMP + 16 * ij)
                dve.tensor_copy(lse_row[:], pLSE).then_inc(S["lse_copied"], 1)

            def over_groups(op, ij, first, second):
                for g, done in ((1, first), (2, second)):
                    src = e[:, 0] if g == 1 else mx
                    dve.tensor_tensor(shaped(mx, g, "token"), shaped(src, g, "token"), token_order(e[:, g], g), op)
                    dve.tensor_tensor(mx[:, NP_:T], src[:, NP_:T], e[:, g, NP_:T], op).then_inc(S[done], 1)
                    if done == first:
                        dve.wait_ge(S[first], BUMP + ij + 1)

            def max_lse(ij):
                dve.wait_ge(S["e_loaded"], BUMP + 16 * (3 * (ij + 1)))
                over_groups(ALU.max, ij, "mx_a", "mxd")

            def denominators(ij):
                dve.wait_ge(S["ex"], BUMP + ij + 1)
                over_groups(ALU.add, ij, "den_a", "den")
                dve.wait_ge(S["den"], BUMP + ij + 1)

            def invert(ij, c):
                dve.reciprocal(mx[:, c * CH:(c + 1) * CH], mx[:, c * CH:(c + 1) * CH]).then_inc(S["rec"], 1)

            def combine(ij, part):
                if part == 0:
                    dve.wait_ge(S["prod"], BUMP + 3 * (ij + 1))
                    dve.wait_ge(S["rec"], BUMP + 3 * (ij + 1))
                g, done = ((1, "comb_a"), (2, "comb_b"))[part]
                dve.tensor_tensor(shaped(o0, g, "token"), shaped(o0, g, "token"), token_order(o[g], g), ALU.add)
                dve.tensor_tensor(o0[:, NP_:T], o0[:, NP_:T], o[g][:, NP_:T], ALU.add).then_inc(S[done], 1)
                dve.wait_ge(S[done], BUMP + ij + 1)
                if part == 1:
                    dve.tensor_tensor(o0[:], o0[:], mx[:], ALU.mult).then_inc(S["comb"], 1)

            def body(cur, nxt, i):
                if nxt is not None and i == 0:
                    split_lo(3 * nxt[0] + nxt[1])
                if cur is not None and 0 <= i - 3 < PAIRS:
                    scale_probs(*cur, i - 3)
                lag = lagging(cur, nxt, i, 1)
                if lag is not None:
                    normalise(*lag)
                if nxt is not None:
                    copy_tile(9 * (3 * nxt[0] + nxt[1]) + i, nxt[1], i)
                if cur is not None:
                    if 0 <= i - 2 < PAIRS:
                        maxima(*cur, i - 2)
                    if 0 <= i - 4:
                        copy_out(*cur, i - 4)
                    j, g = cur
                    if g == 0 and i == 1:
                        lse_rows(j)
                    if g == 0 and i == 3:
                        max_lse(j)
                    if g == 0 and i == 8:
                        denominators(j)
                        invert(j, 0)
                    if g == 1 and i < 2:
                        invert(j, i + 1)
                    if g == 1 and i in (2, 3):
                        combine(j, i - 2)

            dve.wait_ge(S["init"], BUMP + 9)
            dve.wait_ge(S["once"], BUMP + 16 * 3)
            dve.tensor_scalar(gq[:], gq[:], SCALE * HD ** 0.5, None, ALU.mult).then_inc(S["init2"], 1)
            dve.tensor_scalar(gk[:], gk[:], HD ** 0.5, None, ALU.mult).then_inc(S["init2"], 1)
            dve.wait_ge(S["init2"], BUMP + 2)
            walk(dve, body)
            lse_rows(HG)
            max_lse(HG)
            dve.wait_ge(S["mxd"], BUMP + HG + 1)
            dve.tensor_tensor(e[:, 0], e[:, 0], mx[:], ALU.subtract).then_inc(S["sub"], 1)
            for g in (1, 2):
                eg = shaped(e[:, g], g, "group")
                dve.tensor_tensor(eg, eg, group_order(mx, g), ALU.subtract).then_inc(S["sub"], 1)
                dve.tensor_tensor(e[:, g, NP_:T], e[:, g, NP_:T], mx[:, NP_:T], ALU.subtract).then_inc(S["sub"], 1)
            denominators(HG)
            for c in range(NCH):
                invert(HG, c)
            combine(HG, 0)
            combine(HG, 1)

        @block.tensor
        def _(pe):
            pe.wait_ge(S["init"], BUMP + 9)

            def project(step, i):
                q, g = 3 * step[0] + step[1], step[1]
                n = 9 * q + i
                pe.wait_ge(S["tok_copied"], BUMP + n - 2)
                first = True
                for k in range(KD):
                    if i == 0:
                        pe.wait_ge(S["wlo"], BUMP + 8 * q + k + 1)
                    for x, w in ((act_lo, w_hi), (act_hi, w_hi), (act_hi, w_lo)):
                        last = k == KD - 1 and w is w_lo
                        ins = pe.matmul(pj[i % 3][:, 0:3 * HD], tile_cols(x, k, g, i), w[:, k], start=first, stop=last)
                        first = False
                ins.then_inc(S["proj"], 1)

            def transpose_qk(tau, step, i):
                sl = i % 3
                pe.wait_ge(S["normed"], BUMP + tau + 1)
                pe.wait_ge(S["qkt_ready"], BUMP + tau)
                pe.transpose(ptq[:, 0:P], qk[:, sl, 0], ident[:])
                pe.transpose(ptq[:, P:2 * P], ktok[:, i], ident[:]).then_inc(S["qkt_psum"], 1)

            def logits(j, g, p):
                s = 3 * j + g
                n = PAIRS * s + p
                pe.wait_ge(S["max_done"], BUMP + n)
                if p == PAIRS - 1:
                    pe.wait_ge(S["lt_ready"], BUMP + s + 1)
                    pe.matmul(pSS[:, 0:NS], qkt[g][:, 0, NP_:T], qkt[g][:, 1, NP_:T], start=True, stop=True)
                    ins = pe.transpose(pSS[:, NS:NS + CK[g]], lt_s[0:CK[g], :], ident[0:CK[g], 0:CK[g]])
                else:
                    pe.wait_ge(S["qkt_ready"], BUMP + 9 * s + 2 * p + 2)
                    for x, u in enumerate(pair_units(p)):
                        first, nb = keys(g, u)
                        ins = pe.matmul(pS[:, x * 256:x * 256 + nb * P], qkt[g][:, 0, u * P:(u + 1) * P],
                                        qkt[g][:, 1, first * P:(first + nb) * P], start=True, stop=True)
                ins.then_inc(S["s_psum"], 1)

            def cached_logits(j, g, pc):
                s = 3 * j + g
                pe.wait_ge(S[f"kc{pc % 2}_loaded"], BUMP + 16 * (2 * s + pc // 2 + 1))
                if pc == 0:
                    pe.wait_ge(S["qkt_ready"], BUMP + 9 * s + 9)
                    pe.wait_ge(S["max_done"], BUMP + PAIRS * s)
                    pe.wait_ge(S["lse_copied"], BUMP + j + 1)
                n = CSLOT[g] // 4
                w = 8 // n
                for c in range(n):
                    at = 8 * pc + c * w
                    ins = pe.matmul(pLT[0:CK[g], at:at + w], kc[:, pc % 2, c, 0:CK[g]], qkt[g][:, 0, NP_ + at:NP_ + at + w],
                                    start=True, stop=True)
                ins.then_inc(S["kc_used"], 1)

            def transpose_probs(j, g, p):
                n = PAIRS * (3 * j + g) + p
                pe.wait_ge(S["p_norm"], BUMP + n + 1)
                pe.wait_ge(S["pt_ready"], BUMP + n)
                if p == PAIRS - 1:
                    pe.transpose(pPT[0:NS, P:2 * P], L[:, p % 2, 0, 0:NS], ident[:])
                    ins = pe.transpose(pPT[0:CK[g], 0:P], L[:, p % 2, 0, NS:NS + CK[g]], ident[:])
                else:
                    for at, (x, u, b, key, nb) in enumerate(blocks(g, p)):
                        ins = pe.transpose(pPT[:, at * P:(at + 1) * P], L[:, p % 2, x, b * P:(b + 1) * P], ident[:])
                ins.then_inc(S["pt_psum"], 1)

            def values(j, g, p):
                n = PAIRS * (3 * j + g) + p
                pe.wait_ge(S["pt_ready"], BUMP + n + 1)
                pe.wait_ge(S["o_ready"], BUMP + n)
                if p == PAIRS - 1:
                    pe.wait_ge(S["vc_loaded"], BUMP + 16 * total(V_DMAS, j, g))
                    pe.matmul(pO[:, 0:NS], v[g][0:NS, TL], pt[0:NS, 1, 0:NS], start=True, stop=False, skip_group_check=True)
                    w = NS // CSLOT[g]
                    for c in range(CSLOT[g]):
                        vals = (vc if c < 16 else vc2)[0:CK[g], c % 16]
                        ins = pe.matmul(pO[:, c * w:(c + 1) * w], vals, pt[0:CK[g], 0, c * w:(c + 1) * w],
                                        start=False, stop=True, skip_group_check=True)
                else:
                    for at, (x, u, b, key, nb) in enumerate(blocks(g, p)):
                        ins = pe.matmul(pO[:, x * P:(x + 1) * P], v[g][:, key], pt[:, at], start=b == 0, stop=b == nb - 1)
                ins.then_inc(S["o_psum"], 1)

            def lse_transpose(ij):
                pe.wait_ge(S["lse_done"], BUMP + ij + 1)
                pe.wait_ge(S["max_done"], BUMP + 15 * ij)
                pe.transpose(pLSE, lse[:], ident[:]).then_inc(S["lse_psum"], 1)

            def body(cur, nxt, i):
                if nxt is not None:
                    project(nxt, i)
                lag = lagging(cur, nxt, i, 2)
                if lag is not None:
                    transpose_qk(*lag)
                if cur is not None:
                    if cur[1] == 0 and i == 1:
                        lse_transpose(cur[0])
                    if 0 <= i - 2 < 4:
                        cached_logits(*cur, i - 2)
                    if 0 <= i - 2 < PAIRS:
                        logits(*cur, i - 2)
                    if 0 <= i - 3 < PAIRS:
                        transpose_probs(*cur, i - 3)
                    if 0 <= i - 4:
                        values(*cur, i - 4)

            walk(pe, body)
            lse_transpose(HG)


def dense(nc, ctx, a, shared):
    cursor = shared["cursor"]
    alloc, sem, ones, vec, clam, c_eps, vcol = \
        shared["alloc"], shared["sem"], shared["ones"], shared["vec"], shared["clam"], shared["c_eps"], shared["vcol"]
    act_hi, act_lo, att_dram, act_at = shared["act_hi"], shared["act_lo"], shared["att_dram"], shared["act_at"]

    X = alloc("x_res", [P, KD, T])
    b_hi_at = cursor[0]
    b_hi = alloc("b_hi", [P, KD, T], F32R)
    b_lo_at = cursor[0]
    b_lo = alloc("b_lo", [P, KD, T], F32R)
    w_raw = alloc("w_raw", [P, 2, KD, P])
    w_hi = alloc("w_hi", [P, 2, KD, P], F32R)
    w_lo = alloc("w_lo", [P, 2, KD, P], F32R)
    G = [alloc(f"tmp{n}", [P, T]) for n in range(4)]
    assert cursor[0] <= 229344, cursor[0]
    Z = nc.alloc_sbuf_tensor_at("z", [P, KD, T], F32, offset=b_lo_at)
    at = [b_hi_at]

    def sub(name, shape, dt=F32):
        t = nc.alloc_sbuf_tensor_at(name, shape, dt, offset=at[0])
        at[0] += (4 * int(np.prod(shape[1:])) + 31) // 32 * 32
        assert at[0] <= b_lo_at
        return t

    prm = sub("lru_prm", [P, 2, 39])
    tmp8 = sub("tmp8", [P, DB])
    xcat = sub("xcat", [P, 3 + NP_])
    xcat_s = sub("xcat_s", [P, DB, 3 + DS])
    xc = sub("xc", [P, T])
    xc_hi = sub("xc_hi", [P, T], F32R)
    xc_lo = sub("xc_lo", [P, T], F32R)
    ra = sub("ra", [P, T])
    ri = sub("ri", [P, T])
    gel = [G[2], sub("gelu1", [P, T])]
    g_raw = sub("g_raw", [P, 2, P])
    g_hi = sub("g_hi", [P, 2, P], F32R)
    g_lo = sub("g_lo", [P, 2, P], F32R)
    so = nc.alloc_sbuf_tensor_at("st_out_buf", [P, 2, 36], F32, offset=shared["ident_at"])
    p_hi = nc.alloc_sbuf_tensor_at("p_hi", [P, 2, T], F32R, offset=act_at)
    p_lo = nc.alloc_sbuf_tensor_at("p_lo", [P, 2, T], F32R, offset=act_at + 4 * 2 * T)
    p_raw = nc.alloc_sbuf_tensor_at("p_raw", [P, 2, T], F32, offset=act_at + 4 * 4 * T)
    pe_out = nc.alloc_sbuf_tensor_at("pe_out", [P, KD, T], F32, offset=act_at + 4 * 6 * T)

    AO, LRU, BO, WO, MLP, PIN, GT = range(7)
    N0 = [0, 16, 32, 48, 56, 120, 122]
    T0 = [0, 16, 48, 64, 72, 136, 144]
    FB = 4
    PKD = 2

    S = {}
    for n in ("w0_loaded w1_loaded att0_loaded att1_loaded att2_loaded att3_loaded x0_loaded x1_loaded g_loaded "
              "prm0_loaded prm1_loaded p0_loaded p1_loaded y_stored st0_stored st1_stored").split():
        S[n] = sem("d_" + n)
    for n in ("whi wlo mm ev0 ev1 att_hi att_lo init "
              "ghi glo cv rows xc_hi xc_lo la ex_a th den rec qd root_b ix bd h0m h0a h0z scan z save "
              "z_hi z_lo u u_hi u_lo "
              "sqr ssq b_hi b_lo tot root rstd "
              "hid hid_hi hid_lo p_hi p_lo sg gp y").split():
        S[n] = sem("d_" + n)

    with nc.Block() as bump:
        @bump.sync
        def _(sp):
            for x in S.values():
                sp.sem_inc(x, BUMP)

    ps = [ctx.enter_context(nc.psum_tensor(f"d_ps{s}", [P, NCH, 512], F32)) for s in range(2)]
    tot = ctx.enter_context(nc.psum_tensor("d_tot", [P, 2, 512], F32))
    block = ctx.enter_context(nc.Block())

    def out3(s):
        return ps[s][:, :, 0:CH]

    def c3(ap):
        return ap.rearrange("p (c t) -> p c t", c=NCH)

    def c2(ap):
        return ap.rearrange("p (c t) -> p c t", c=2)

    def seq(ap):
        return ap.rearrange("p (b t) -> p b t", b=DB)

    @block.sync
    def _(sp):
        def load_w(n, slot, nth):
            sp.wait_ge(S["whi"], BUMP + n - 1)
            sp.wait_ge(S["wlo"], BUMP + n - 1)
            sp.dma_start(w_raw[:, slot], a["w_stream"][nth].rearrange("p (k c) -> p k c", k=KD)).then_inc(S[f"w{slot}_loaded"], 16)

        def load_oa(m):
            sp.wait_ge(S["whi"], BUMP + 2 * m)
            sp.wait_ge(S["wlo"], BUMP + 2 * m)
            sp.dma_start(w_raw[:, 1, 0:HG], a["w_oa_t"][m].rearrange("p (k c) -> p k c", k=HG)).then_inc(S["w1_loaded"], 16)

        def load_lru(m, y):
            for s in range(2):
                load_w(N0[LRU] + 2 * m + s, s, KD + 2 * m + s)
            sp.wait_ge(S["mm"], BUMP + T0[LRU])
            sp.wait_ge(S["save"], BUMP + m - 1)
            sp.wait_ge(S["z"], BUMP + m - 1)
            sp.dma_start(prm[:, y], a["lru_prm"][m]).then_inc(S[f"prm{y}_loaded"], 16)
            sp.wait_ge(S["ghi"], BUMP + m)
            sp.wait_ge(S["glo"], BUMP + m)
            sp.dma_start(g_raw[:], a["w_gates"][m]).then_inc(S["g_loaded"], 16)

        def store_state(m, y):
            sp.wait_ge(S["rows"], BUMP + m + 1)
            sp.wait_ge(S["save"], BUMP + m + 1)
            sp.dma_start(a["st_out"][m], so[:, y]).then_inc(S[f"st{y}_stored"], 16)

        load_w(0, 0, 0)
        load_oa(0)
        for j in range(HG):
            sp.dma_start(G[j][:], att_dram[j + 1]).then_inc(S[f"att{j}_loaded"], 16)
        with sp.Fori(1, KD, 1) as m:
            load_w(2 * m, 0, m)
            load_oa(m)
        for y in range(2):
            load_lru(y, y)
        with sp.Fori(1, KD // 2, 1) as x:
            for y in range(2):
                load_lru(2 * x + y, y)
                store_state(2 * x + y - 2, y)
        with sp.Fori(0, KD, 1) as m:
            for s in range(2):
                load_w(N0[BO] + 2 * m + s, s, 3 * KD + 2 * m + s)
        for y in range(2):
            store_state(KD - 2 + y, y)
        for s in range(2):
            load_w(N0[WO] + s, s, 5 * KD + s)
        sp.wait_ge(S["u"], BUMP + KD)
        for m in range(KD):
            if m >= 2:
                sp.wait_ge(S[f"ev{m % 2}"], BUMP + (T0[WO] + m - 2) // 2 + 1)
            sp.dma_start(G[2 + m % 2][:], a["x_t"][:, m]).then_inc(S[f"x{m % 2}_loaded"], 16)
            if m + 2 < KD:
                load_w(N0[WO] + m + 2, m % 2, 5 * KD + m + 2)
        with sp.Fori(0, FB * KD, 1) as x:
            for s in range(2):
                load_w(N0[MLP] + 2 * x + s, s, 6 * KD + 2 * x + s)
        for s in range(2):
            load_w(N0[PIN] + s, s, N0[PIN] - KD + s)
        sp.wait_ge(S["mm"], BUMP + T0[PIN])
        for k in range(PKD):
            sp.dma_start(p_raw[:, k], a["p_t"][:, k]).then_inc(S[f"p{k}_loaded"], 16)
        for m in range(KD):
            load_w(N0[GT] + m, m % 2, N0[GT] - KD + m)
        for m in range(KD):
            sp.wait_ge(S["y"], BUMP + m + 1)
            sp.dma_start(a["y_t"][:, m], X[:, m]).then_inc(S["y_stored"], 16)
        sp.wait_ge(S["y_stored"], BUMP + 16 * KD)
        for y in range(2):
            sp.wait_ge(S[f"st{y}_stored"], BUMP + 16 * (KD // 2))

    @block.tensor
    def _(pe):
        def product(s, n, slot, hi, lo, free, nk=KD, k0=0, ready=None):
            pe.wait_ge(S["wlo"], BUMP + n + 1)
            pe.wait_ge(S[f"ev{s}"], BUMP + free)
            for k in range(nk):
                if ready is not None:
                    pe.wait_ge(S[ready[0]], BUMP + ready[1] + k + 1)
                for w, x in ((w_hi, lo), (w_hi, hi), (w_lo, hi)):
                    for c in range(NCH):
                        ins = pe.matmul(ps[s][:, c, 0:CH], w[:, slot, k0 + k], x[:, k, c * CH:(c + 1) * CH],
                                        start=k == 0 and x is lo, stop=k == nk - 1 and w is w_lo)
            ins.then_inc(S["mm"], 1)

        def column_sums(r):
            pe.wait_ge(S["ssq"], BUMP + KD * (r + 1))
            for c in range(NCH):
                pe.wait_ge(S["root"], BUMP + NCH * r + max(c - 1, 0))
                pe.matmul(tot[:, c % 2, 0:CH], ones[:], G[1][:, c * CH:(c + 1) * CH], start=True, stop=True).then_inc(S["tot"], 1)

        with pe.Fori(0, KD, 1) as m:
            product(0, 2 * m, 0, act_hi, act_lo, m)
            product(1, 2 * m + 1, 1, b_hi, b_lo, m, nk=HG, ready=("att_lo", 0))
        with pe.Fori(0, KD, 1) as m:
            for s in range(2):
                product(s, N0[LRU] + 2 * m + s, s, act_hi, act_lo, T0[LRU] // 2 + 2 * m)
            pe.wait_ge(S["xc_lo"], BUMP + m + 1)
            pe.wait_ge(S["glo"], BUMP + m + 1)
            for s in range(2):
                pe.wait_ge(S[f"ev{s}"], BUMP + T0[LRU] // 2 + 2 * m + 1)
                for w, x in ((g_hi, xc_lo), (g_hi, xc_hi), (g_lo, xc_hi)):
                    for c in range(NCH):
                        ins = pe.matmul(ps[s][:, c, 0:CH], w[:, s], x[:, c * CH:(c + 1) * CH],
                                        start=x is xc_lo, stop=w is g_lo)
                ins.then_inc(S["mm"], 1)
        with pe.Fori(0, KD, 1) as m:
            product(0, N0[BO] + 2 * m, 0, act_hi, act_lo, T0[BO] // 2 + m)
            product(1, N0[BO] + 2 * m + 1, 1, b_hi, b_lo, T0[BO] // 2 + m, ready=("z_lo", 0))
        for m in range(KD):
            product(m % 2, N0[WO] + m, m % 2, act_hi, act_lo, (T0[WO] + m) // 2, ready=("u_lo", 0))
        column_sums(0)
        with pe.Fori(0, FB, 1) as kb:
            for i in range(2 * KD):
                hi, lo, ready = (b_hi, b_lo, ("b_lo", 0)) if i < KD else (act_hi, act_lo, ("hid_lo", KD * kb))
                product(i % 2, N0[MLP] + 16 * kb + i, i % 2, hi, lo, T0[MLP] // 2 + 8 * kb + i // 2, ready=ready)
        for i in range(KD):
            product(i % 2, N0[PIN] + i // 4, i // 4, p_hi, p_lo, (T0[PIN] + i) // 2, nk=PKD, k0=PKD * (i % 4),
                    ready=("p_lo", 0))
        for m in range(KD):
            if m == 1:
                column_sums(1)
            product(m % 2, N0[GT] + m, m % 2, b_hi, b_lo, (T0[GT] + m) // 2, ready=("b_lo", KD))

    def walk(eng, split, step):
        split(0, 0, 0)
        step("attention", 0, 0)
        with eng.Fori(0, KD, 1) as m:
            split(m, 1, T0[AO] + 2 * m, HG)
            step("gate_a", m, 0)
            split(m + 1, 0, T0[AO] + 2 * m + 1)
            step("merge_a", m, 0)
        step("lru_start", 0, 0)
        with eng.Fori(0, KD // 2, 1) as x:
            for y in range(2):
                m = 2 * x + y
                split(N0[LRU] // 2 + m, 1, T0[LRU] + 4 * m)
                step("xb", m, y, x)
                split(N0[LRU] // 2 + m + 1, 0, T0[LRU] + 4 * m + 1)
                step("yb", m, y, x)
                step("lru", m, y, x)
        step("z_split", 0, 0)
        with eng.Fori(0, KD, 1) as m:
            split(N0[BO] // 2 + m, 1, T0[BO] + 2 * m)
            step("gate_b", m, 0)
            split(N0[BO] // 2 + m + 1, 0, T0[BO] + 2 * m + 1)
            step("merge_b", m, 0)
        step("u_split", 0, 0)
        for m in range(KD):
            split((N0[WO] + m + 1) // 2, (m + 1) % 2, T0[WO] + m)
            step("wo", m, m)
        step("rms", 0, 0)
        with eng.Fori(0, FB, 1) as kb:
            for i in range(2 * KD):
                split(N0[MLP] // 2 + 8 * kb + (i + 1) // 2, (i + 1) % 2, T0[MLP] + 16 * kb + i)
                step("up" if i < KD else "down", kb, i)
        step("p_split", 0, 0)
        split(N0[PIN] // 2, 1, T0[PIN])
        for m in range(KD):
            if m == KD // 2:
                split(N0[GT] // 2, 0, T0[PIN] + m)
            step("pin", m, m)
            step("norm2", m, m)
        step("rms", 1, 1)
        for m in range(KD):
            if m < KD - 1:
                split((N0[GT] + m + 1) // 2, (m + 1) % 2, T0[GT] + m)
            step("gate_p", m, m)

    @block.scalar
    def _(act):
        def split(x, s, after, nk=KD):
            act.wait_ge(S["mm"], BUMP + after)
            act.wait_ge(S[f"w{s}_loaded"], BUMP + 16 * (x + 1))
            act.activation(w_hi[:, s, 0:nk], w_raw[:, s, 0:nk], ACT.Copy).then_inc(S["whi"], 1)

        def split_in(name, n, dst, src):
            for k in range(n):
                act.activation(dst[:, k], src[:, k], ACT.Copy).then_inc(S[name], 1)

        def squares(m, r):
            act.wait_ge(S["ssq"], BUMP + KD * r + m)
            act.activation(G[0][:], X[:, m], ACT.Square).then_inc(S["sqr"], 1)
            act.activation(b_hi[:, m], X[:, m], ACT.Copy, scale=vcol("g_ple" if r else "g_mlp", m)).then_inc(S["b_hi"], 1)

        def step(name, m, y, x=None):
            if name == "attention":
                for j in range(HG):
                    act.wait_ge(S[f"att{j}_loaded"], BUMP + 16 * 1)
                    act.activation(b_hi[:, j], G[j][:], ACT.Copy).then_inc(S["att_hi"], 1)
                act.wait_ge(S["att_lo"], BUMP + HG)
            elif name in ("gate_a", "gate_b"):
                t0 = T0[AO] if name == "gate_a" else T0[BO]
                act.wait_ge(S["ev1"], BUMP + t0 // 2 + m)
                act.wait_ge(S["mm"], BUMP + t0 + 2 * m + 1)
                act.activation(c3(G[0][:]), out3(0), ACT.Sigmoid).then_inc(S["ev0"], 1)
            elif name == "xb":
                act.wait_ge(S["g_loaded"], BUMP + 16 * (m + 1))
                act.wait_ge(S["mm"], BUMP + T0[LRU] + 4 * m)
                act.activation(g_hi[:], g_raw[:], ACT.Copy).then_inc(S["ghi"], 1)
                act.wait_ge(S[f"prm{y}_loaded"], BUMP + 16 * (x + 1))
                act.wait_ge(S["cv"], BUMP + 4 * m)
                act.wait_ge(S["rows"], BUMP + m)
                act.activation(xcat_s[:, :, 0:3], seq(prm[:, y, 7:31]), ACT.Copy)
                act.wait_ge(S["mm"], BUMP + T0[LRU] + 4 * m + 1)
                act.activation(c2(xcat[:, 3:3 + 2 * CH]), ps[0][:, 0:2, 0:CH], ACT.Copy)
                act.activation(xcat[:, 3 + 2 * CH:3 + NP_], ps[0][:, 2, 0:NP_ - 2 * CH], ACT.Copy)
                act.activation(xcat_s[:, :, 3:3 + DS], seq(ps[0][:, 2, NP_ - 2 * CH:CH]), ACT.Copy).then_inc(S["ev0"], 1)
                act.wait_ge(S["ev0"], BUMP + T0[LRU] // 2 + 2 * m + 1)
                act.wait_ge(S[f"st{y}_stored"], BUMP + 16 * x)
                act.activation(so[:, y, 0:3], xcat[:, NP_:NP_ + 3], ACT.Copy)
                act.activation(seq(so[:, y, 3:27]), xcat_s[:, :, DS:DS + 3], ACT.Copy).then_inc(S["rows"], 1)
            elif name == "yb":
                act.wait_ge(S["cv"], BUMP + 4 * (m + 1))
                act.activation(xc_hi[:], xc[:], ACT.Copy).then_inc(S["xc_hi"], 1)
                act.wait_ge(S["z"], BUMP + m - 1)
                act.wait_ge(S["mm"], BUMP + T0[LRU] + 4 * m + 1 + 1)
                act.activation(c3(gel[y][:]), out3(1), ACT.Gelu_apprx_tanh).then_inc(S["ev1"], 1)
            elif name == "lru":
                t = T0[LRU] + 4 * m + 2
                act.wait_ge(S["root_b"], BUMP + m)
                act.wait_ge(S["bd"], BUMP + m)
                act.wait_ge(S["mm"], BUMP + t + 1)
                act.activation(c3(ra[:]), out3(0), ACT.Sigmoid, bias=prm[:, y, 1:2]).then_inc(S["ev0"], 1)
                act.wait_ge(S["mm"], BUMP + t + 1 + 1)
                act.activation(c3(ri[:]), out3(1), ACT.Sigmoid, bias=prm[:, y, 2:3]).then_inc(S["ev1"], 1)
                act.wait_ge(S["la"], BUMP + m + 1)
                act.wait_ge(S["scan"], BUMP + m)
                act.activation(G[0][:], G[3][:], ACT.Exp).then_inc(S["ex_a"], 1)
                act.wait_ge(S["ex_a"], BUMP + m + 1)
                act.activation(G[3][:], G[3][:], ACT.Tanh, scale=-1.0).then_inc(S["th"], 1)
                act.wait_ge(S["qd"], BUMP + m + 1)
                act.activation(G[3][:], ra[:], ACT.Sqrt).then_inc(S["root_b"], 1)
            elif name == "z_split":
                act.wait_ge(S["z"], BUMP + KD)
                act.wait_ge(S["mm"], BUMP + T0[BO])
                act.wait_ge(S["rows"], BUMP + KD)
                split_in("z_hi", KD, b_hi, Z)
            elif name == "u_split":
                act.wait_ge(S["u"], BUMP + KD)
                act.wait_ge(S["mm"], BUMP + T0[WO])
                split_in("u_hi", KD, act_hi, X)
            elif name == "wo":
                act.wait_ge(S[f"ev{m % 2}"], BUMP + (T0[WO] + m) // 2 + 1)
                squares(m, 0)
            elif name == "norm2":
                if m == 0:
                    act.wait_ge(S["ev0"], BUMP + T0[PIN] // 2)
                    act.wait_ge(S["ev1"], BUMP + T0[PIN] // 2)
                squares(m, 1)
            elif name == "rms":
                act.wait_ge(S["ev0"], BUMP + (T0[PIN] // 2 if m else T0[MLP] // 2))
                act.wait_ge(S["ev1"], BUMP + (T0[PIN] // 2 if m else T0[MLP] // 2))
                for c in range(NCH):
                    act.wait_ge(S["tot"], BUMP + NCH * m + c + 1)
                    act.activation(G[3][:, c * CH:(c + 1) * CH], tot[:, c % 2, 0:CH], ACT.Sqrt, bias=c_eps[:], scale=1.0 / D).then_inc(S["root"], 1)
            elif name == "up":
                act.wait_ge(S["hid"], BUMP + KD * m + y + 1)
                act.activation(act_hi[:, y], G[2 * (y % 2)][:], ACT.Copy).then_inc(S["hid_hi"], 1)
            elif name == "p_split":
                for k in range(PKD):
                    act.wait_ge(S[f"p{k}_loaded"], BUMP + 16 * 1)
                    act.activation(p_hi[:, k], p_raw[:, k], ACT.Copy).then_inc(S["p_hi"], 1)
            elif name == "pin":
                act.wait_ge(S["mm"], BUMP + T0[PIN] + m + 1)
                act.activation(c3(pe_out[:, m]), out3(m % 2), ACT.Copy).then_inc(S[f"ev{m % 2}"], 1)
            elif name == "gate_p":
                act.wait_ge(S[f"ev{m % 2}"], BUMP + (T0[GT] + m) // 2 + 1)
                act.activation(G[2 * (m % 2)][:], G[2 * (m % 2)][:], ACT.Sigmoid).then_inc(S["sg"], 1)

        walk(act, split, step)

    @block.gpsimd
    def _(pool):
        def split(x, s, after, nk=KD):
            pool.wait_ge(S["whi"], BUMP + 2 * x + s + 1)
            pool.tensor_tensor(w_lo[:, s, 0:nk], w_raw[:, s, 0:nk], w_hi[:, s, 0:nk].bitcast(F32), ALU.subtract).then_inc(S["wlo"], 1)

        def step(name, m, y, x=None):
            if name == "lru_start":
                pool.wait_ge(S["mm"], BUMP + T0[LRU])
                pool.memset(xcat[:, 0:3], 0.0).then_inc(S["init"], 1)
            elif name == "xb":
                pool.wait_ge(S["ghi"], BUMP + m + 1)
                pool.tensor_tensor(g_lo[:], g_raw[:], g_hi[:].bitcast(F32), ALU.subtract).then_inc(S["glo"], 1)
            elif name == "yb":
                pool.wait_ge(S["xc_hi"], BUMP + m + 1)
                pool.tensor_tensor(xc_lo[:], xc[:], xc_hi[:].bitcast(F32), ALU.subtract).then_inc(S["xc_lo"], 1)
            elif name == "lru":
                pool.wait_ge(S["ev1"], BUMP + T0[LRU] // 2 + 2 * m + 2)
                pool.tensor_tensor(ri[:], ri[:], xc[:], ALU.mult).then_inc(S["ix"], 1)
            elif name in ("wo", "norm2"):
                r = 1 if name == "norm2" else 0
                pool.wait_ge(S["sqr"], BUMP + KD * r + m + 1)
                pool.wait_ge(S["ssq"], BUMP + KD * r + m)
                if m == 0:
                    pool.wait_ge(S["tot"], BUMP + NCH * r)
                    pool.tensor_copy(G[1][:], G[0][:]).then_inc(S["ssq"], 1)
                else:
                    pool.tensor_tensor(G[1][:], G[1][:], G[0][:], ALU.add).then_inc(S["ssq"], 1)
            elif name == "up":
                pool.wait_ge(S["hid_hi"], BUMP + KD * m + y + 1)
                g = G[2 * (y % 2)]
                pool.tensor_tensor(act_lo[:, y], g[:], act_hi[:, y].bitcast(F32), ALU.subtract).then_inc(S["hid_lo"], 1)

        walk(pool, split, step)

    @block.vector
    def _(dve):
        def lo_part(name, n, dst, src, hi, hi_ready):
            for k in range(n):
                dve.wait_ge(S[hi_ready], BUMP + k + 1)
                dve.tensor_tensor(dst[:, k], src[:, k], hi[:, k].bitcast(F32), ALU.subtract).then_inc(S[name], 1)

        def scaled_lo(m, r):
            dve.wait_ge(S["b_hi"], BUMP + KD * r + m + 1)
            dve.scalar_tensor_tensor(out=b_lo[:, m], in0=X[:, m], scalar=vcol("g_ple" if r else "g_mlp", m),
                                     in1=b_hi[:, m].bitcast(F32), op0=ALU.mult, op1=ALU.subtract).then_inc(S["b_lo"], 1)

        def step(name, m, y, x=None):
            if name == "attention":
                for j in range(HG):
                    dve.wait_ge(S["att_hi"], BUMP + j + 1)
                    dve.tensor_tensor(b_lo[:, j], G[j][:], b_hi[:, j].bitcast(F32), ALU.subtract).then_inc(S["att_lo"], 1)
            elif name == "merge_a":
                dve.wait_ge(S["ev0"], BUMP + T0[AO] // 2 + m + 1)
                dve.wait_ge(S["mm"], BUMP + T0[AO] + 2 * m + 1 + 1)
                dve.tensor_tensor(c3(X[:, m]), c3(G[0][:]), out3(1), ALU.mult).then_inc(S["ev1"], 1)
            elif name == "xb":
                was = T0[LRU] // 2 + 2 * m
                w = prm[:, y, 3:7]
                dve.wait_ge(S["ev0"], BUMP + was + 1)
                dve.wait_ge(S["ix"], BUMP + m)
                dve.wait_ge(S["xc_lo"], BUMP + m)
                dve.wait_ge(S["init"], BUMP + 1)
                dve.tensor_scalar(xc[:, 0:NP_], xcat[:, 0:NP_], w[:, 0:1], prm[:, y, 0:1], ALU.mult, ALU.add)
                dve.tensor_scalar(seq(xc[:, NP_:T]), xcat_s[:, :, 0:DS], w[:, 0:1], prm[:, y, 0:1], ALU.mult, ALU.add).then_inc(S["cv"], 1)
                for j in range(1, 4):
                    dve.wait_ge(S["cv"], BUMP + 4 * m + j)
                    dve.scalar_tensor_tensor(out=xc[:, 0:NP_], in0=xcat[:, j:j + NP_], scalar=w[:, j:j + 1], in1=xc[:, 0:NP_],
                                             op0=ALU.mult, op1=ALU.add)
                    dve.scalar_tensor_tensor(out=seq(xc[:, NP_:T]), in0=xcat_s[:, :, j:j + DS], scalar=w[:, j:j + 1],
                                             in1=seq(xc[:, NP_:T]), op0=ALU.mult, op1=ALU.add).then_inc(S["cv"], 1)
            elif name == "lru":
                was = T0[LRU] // 2 + 2 * m + 1
                dve.wait_ge(S["ev0"], BUMP + was + 1)
                dve.wait_ge(S["bd"], BUMP + m)
                dve.tensor_scalar(G[3][:], ra[:], clam[:].rearrange("p (k o) -> p k o", o=1)[:, m], None, ALU.mult).then_inc(S["la"], 1)
                dve.wait_ge(S["ex_a"], BUMP + m + 1)
                dve.tensor_tensor(ra[:], G[0][:], G[0][:], ALU.mult).then_inc(S["den"], 1)
                dve.wait_ge(S["den"], BUMP + m + 1)
                dve.wait_ge(S["th"], BUMP + m + 1)
                dve.scalar_tensor_tensor(out=ra[:], in0=ra[:], scalar=1.0, in1=G[3][:], op0=ALU.add, op1=ALU.mult).then_inc(S["qd"], 1)
                first = seq(G[0][:, NP_:T])[:, :, 0]
                dve.tensor_tensor(tmp8[:], first, prm[:, y, 31:39], ALU.mult).then_inc(S["h0m"], 1)
                dve.wait_ge(S["root_b"], BUMP + m + 1)
                dve.wait_ge(S["ix"], BUMP + m + 1)
                dve.tensor_tensor(G[3][:], G[3][:], ri[:], ALU.mult).then_inc(S["bd"], 1)
                dve.wait_ge(S["bd"], BUMP + m + 1)
                dve.wait_ge(S["h0m"], BUMP + m + 1)
                b0 = seq(G[3][:, NP_:T])[:, :, 0]
                dve.tensor_tensor(b0, b0, tmp8[:], ALU.add).then_inc(S["h0a"], 1)
                dve.memset(first, 0.0).then_inc(S["h0z"], 1)
                dve.wait_ge(S["save"], BUMP + m)
                dve.wait_ge(S["h0a"], BUMP + m + 1)
                dve.wait_ge(S["h0z"], BUMP + m + 1)
                dve.tensor_tensor_scan(G[1][:], G[0][:], G[3][:], 0.0, ALU.mult, ALU.add).then_inc(S["scan"], 1)
                dve.wait_ge(S["scan"], BUMP + m + 1)
                dve.wait_ge(S["ev1"], BUMP + was)
                dve.tensor_tensor(Z[:, m], G[1][:], gel[y][:], ALU.mult).then_inc(S["z"], 1)
                dve.wait_ge(S[f"st{y}_stored"], BUMP + 16 * x)
                dve.tensor_copy(so[:, y, 27:28], G[1][:, NP_ - 1:NP_])
                dve.tensor_copy(so[:, y, 28:36], seq(G[1][:, NP_:T])[:, :, DS - 1]).then_inc(S["save"], 1)
            elif name == "z_split":
                lo_part("z_lo", KD, b_lo, Z, b_hi, "z_hi")
            elif name == "merge_b":
                dve.wait_ge(S["save"], BUMP + KD)
                dve.wait_ge(S["u"], BUMP + m)
                dve.wait_ge(S["ev0"], BUMP + T0[BO] // 2 + m + 1)
                dve.wait_ge(S["mm"], BUMP + T0[BO] + 2 * m + 1 + 1)
                dve.tensor_tensor(c3(G[1][:]), c3(G[0][:]), out3(1), ALU.mult).then_inc(S["ev1"], 1)
                dve.wait_ge(S["ev1"], BUMP + T0[BO] // 2 + m + 1)
                dve.tensor_tensor(X[:, m], X[:, m], G[1][:], ALU.add).then_inc(S["u"], 1)
            elif name == "u_split":
                lo_part("u_lo", KD, act_lo, X, act_hi, "u_hi")
            elif name == "wo":
                dve.wait_ge(S[f"x{m % 2}_loaded"], BUMP + 16 * (m // 2 + 1))
                dve.wait_ge(S["u_lo"], BUMP + KD)
                dve.wait_ge(S["mm"], BUMP + T0[WO] + m + 1)
                dve.tensor_tensor(c3(X[:, m]), c3(G[2 + m % 2][:]), out3(m % 2), ALU.add).then_inc(S[f"ev{m % 2}"], 1)
                scaled_lo(m, 0)
            elif name == "norm2":
                scaled_lo(m, 1)
            elif name == "rms":
                for c in range(NCH):
                    dve.wait_ge(S["root"], BUMP + NCH * m + c + 1)
                    r = G[3][:, c * CH:(c + 1) * CH]
                    dve.reciprocal(r, r).then_inc(S["rstd"], 1)
                dve.wait_ge(S["rstd"], BUMP + NCH * (m + 1))
            elif name == "up":
                s, g = y % 2, G[2 * (y % 2)]
                dve.wait_ge(S["hid_lo"], BUMP + KD * m + y - 1)
                dve.wait_ge(S["mm"], BUMP + T0[MLP] + 16 * m + y + 1)
                dve.tensor_tensor(c3(g[:]), out3(s), c3(G[3][:]), ALU.mult).then_inc(S[f"ev{s}"], 1)
                dve.wait_ge(S[f"ev{s}"], BUMP + T0[MLP] // 2 + 8 * m + y // 2 + 1)
                dve.scalar_tensor_tensor(out=g[:], in0=g[:], scalar=0.0, in1=g[:], op0=ALU.max, op1=ALU.mult).then_inc(S["hid"], 1)
            elif name == "down":
                k, s = y - KD, y % 2
                dve.wait_ge(S[f"ev{s}"], BUMP + T0[MLP] // 2 + 8 * m + y // 2)
                dve.wait_ge(S["mm"], BUMP + T0[MLP] + 16 * m + y + 1)
                dve.tensor_tensor(c3(X[:, k]), c3(X[:, k]), out3(s), ALU.add).then_inc(S[f"ev{s}"], 1)
            elif name == "p_split":
                lo_part("p_lo", PKD, p_lo, p_raw, p_hi, "p_hi")
            elif name == "gate_p":
                s, g = m % 2, G[2 * (m % 2)]
                dve.wait_ge(S["mm"], BUMP + T0[GT] + m + 1)
                dve.wait_ge(S["gp"], BUMP + m - 1)
                dve.wait_ge(S["y"], BUMP + m - 1)
                dve.tensor_tensor(c3(g[:]), out3(s), c3(G[3][:]), ALU.mult).then_inc(S[f"ev{s}"], 1)
                dve.wait_ge(S["sg"], BUMP + m + 1)
                dve.tensor_tensor(g[:], g[:], pe_out[:, m], ALU.mult).then_inc(S["gp"], 1)
                dve.wait_ge(S["gp"], BUMP + m + 1)
                dve.tensor_tensor(X[:, m], X[:, m], g[:], ALU.add).then_inc(S["y"], 1)

        walk(dve, lambda x, s, after, nk=KD: None, step)


def tiles(w):
    r, c = w.shape
    return w.reshape(r // P, P, c // P, P).transpose(2, 1, 0, 3).reshape(c // P, P, r)


def feature_major(prompt, sample):
    width = prompt.shape[-1]
    x = np.concatenate([prompt.reshape(NP_, width), sample.reshape(NS, width)], 0)
    return x.T.reshape(width // P, P, T).transpose(1, 0, 2)


def layout(i):
    out = {"x_t": feature_major(i["x_prompt"], i["x_sample"]), "p_t": feature_major(i["p_prompt"], i["p_sample"])}
    names = ("g_mix", "g_mlp", "g_ple", "b_conv", "b_rg_a", "b_rg_i", "lam", "w_conv")
    out["vecs"] = np.concatenate([i[n].reshape(-1, P) for n in names], 0).T
    out["g_q"], out["g_k"] = i["g_q"].reshape(1, HD), i["g_k"].reshape(1, HD)
    out["rel_bias"], out["bias_sel"] = i["rel_bias"], bias_selection()
    of = np.arange(NS) // DS
    out["same_seq"] = np.where(of[:, None] == of[None, :], 0, NEG).astype(np.float32)
    w_in = i["w_in"][0]
    att = 3 * NG * HG * HD
    qkv = w_in[:, :att].reshape(KD, P, 3, NG, HG, HD)
    out["w_qkv"] = qkv.transpose(4, 3, 1, 0, 2, 5).reshape(HG * NG, P, KD, 3 * HD)
    for g, dil in enumerate(DIL):
        c = i[f"cache_kv{g + 1}"][0]
        if g == 0:
            c = c[:, None]
        else:
            c = c.reshape(DB, c.shape[1] // dil, dil, 2, HG, HD)[:, :, 0:DS].transpose(0, 2, 1, 3, 4, 5)
        c = c.reshape(CSLOT[g], CK[g], 2, HG, HD)
        out[f"kc{g}"] = c[:, :, 0].transpose(2, 3, 0, 1)
        out[f"vc{g}"] = c[:, :, 1].transpose(2, 1, 0, 3)
    xb, yb, ga, gb = (tiles(w_in[:, att + D * n:att + D * (n + 1)]) for n in range(4))
    w_down = i["w_down"][0]
    up = tiles(i["w_up"][0]).reshape(4, KD, P, D)
    down = np.stack([tiles(w_down[D * n:D * (n + 1)]) for n in range(4)])
    pin = tiles(i["w_ple_in"][0]).reshape(2, 4, P, D // 4).transpose(0, 2, 1, 3)

    def in_turn(x, y):
        return np.stack([x, y], 1).reshape(2 * KD, P, D)

    out["w_stream"] = np.concatenate([
        ga, in_turn(xb, yb), in_turn(gb, tiles(i["w_ob"][0])), tiles(i["w_o"][0]),
        np.concatenate([up, down], 1).reshape(8 * KD, P, D), pin.reshape(2, P, D), tiles(i["w_ple_gate"][0])], 0)
    out["w_oa_t"] = tiles(i["w_oa"][0])
    gates = np.zeros((KD, P, 2, P), np.float32)
    half = P // 2
    for c, n in enumerate(("w_rg_a", "w_rg_i")):
        w = i[n][0].reshape(KD, 2, half, half)
        for h in range(2):
            gates[:, half * h:half * (h + 1), c, half * h:half * (h + 1)] = w[:, h]
    out["w_gates"] = gates
    rows = [i["b_conv"], i["b_rg_a"], i["b_rg_i"], i["w_conv"][0], i["state_conv"].reshape(-1, D), i["state_lru"].reshape(-1, D)]
    out["lru_prm"] = np.concatenate(rows, 0).reshape(-1, KD, P).transpose(1, 2, 0)
    return {n: np.ascontiguousarray(x) for n, x in out.items()}


def kernel(**inputs):
    import concourse.bacc as bacc
    from concourse.bass_utils import run_bass_kernel_spmd

    arrays = layout({n: np.asarray(x) for n, x in inputs.items()})
    outs = {"y_t": (P, KD, T), "st_out": (KD, P, 36)}
    keep = (P, NP_ // 2, NP_)
    for g in range(NG):
        outs[f"kv{g}_p"], outs[f"kv{g}_s"] = (keep[g], 2, HG, HD), (NS, 2, HG, HD)
    nc = bacc.Bacc("TRN2", target_bir_lowering=False, num_devices=1)
    a = {n: nc.dram_tensor(n, x.shape, mybir.dt.from_np(x.dtype), kind="ExternalInput").ap() for n, x in arrays.items()}
    for n, shape in outs.items():
        a[n] = nc.dram_tensor(n, shape, F32, kind="ExternalOutput").ap()
    build(nc, a)
    r = run_bass_kernel_spmd(nc, [arrays], core_ids=[0]).results[0]

    y = r["y_t"].transpose(2, 1, 0).reshape(T, D)
    state = r["st_out"].transpose(2, 0, 1).reshape(36, D)
    kv_p = [r[f"kv{g}_p"].reshape(1, 1, keep[g], 2, HG, HD) for g in range(NG)]
    kv_s = [r[f"kv{g}_s"].reshape(1, DB, DS, 2, HG, HD) for g in range(NG)]
    return (y[:NP_].reshape(1, NP_, D), y[NP_:].reshape(DB, DS, D), *kv_p, state[0:3].reshape(1, 1, 3, D),
            state[27:28].reshape(1, 1, D), *kv_s, state[3:27].reshape(1, DB, 3, D), state[28:36].reshape(1, DB, D))
```
